# Optimizing a Trainium2 kernel written in Bass

```python
import jax
import jax.numpy as jnp
from jax import lax
import numpy as np

D_MODEL = 1024
BATCH = 1
SEQ = 128
DEPTH = 1
DEC_BATCH = 1
DEC_SEQ = 1024
PAST_LEN = 128

GRID_W = 64
POOL_GROUPS = 4
POOL_GROUP_DIM = D_MODEL // 8
POOL_DIM = POOL_GROUPS * POOL_GROUP_DIM
POOL_WINDOWS = (2, 4, 8, 16)
DN_HEADS = 8
DN_HEAD_DIM = D_MODEL // DN_HEADS
DN_DIM = DN_HEADS * DN_HEAD_DIM
CONV_K = 5
CHUNK = 64
N_BRANCH = 2
N_EXPERTS = 16
EXPERT_DIM = D_MODEL
EC_FACTOR = 2
EPS = 1e-6

OFF_POOL = 0
OFF_Q = OFF_POOL + POOL_DIM
OFF_K = OFF_Q + DN_DIM
OFF_V = OFF_K + DN_DIM
OFF_G = OFF_V + DN_DIM
OFF_BETA = OFF_G + DN_DIM
OFF_ALPHA = OFF_BETA + 2 * DN_HEADS
OFF_MERGE = OFF_ALPHA + 2 * DN_HEADS
IN_COLS = OFF_MERGE + N_BRANCH * D_MODEL

kernel_name = "hybrid_pool_deltanet_ec_diffusion_step"

def rmsnorm(x, g):
    xf = x.astype(jnp.float32)
    y = xf * lax.rsqrt(jnp.mean(xf * xf, axis=-1, keepdims=True) + EPS)
    return (y * g.astype(jnp.float32)).astype(x.dtype)

def l2norm(x):
    return x * lax.rsqrt(jnp.sum(x * x, axis=-1, keepdims=True) + EPS)

def centred_window_mean(x, w, axis):
    L = x.shape[axis]
    cs = jnp.cumsum(x.astype(jnp.float32), axis=axis)
    pad = [(0, 0)] * x.ndim
    pad[axis] = (1, 0)
    cs = jnp.pad(cs, pad)
    t = jnp.arange(L)
    lo = jnp.clip(t - w // 2, 0, L)
    hi = jnp.clip(t + w // 2, 0, L)
    s = jnp.take(cs, hi, axis=axis) - jnp.take(cs, lo, axis=axis)
    shape = [1] * x.ndim
    shape[axis] = L
    cnt = (hi - lo).astype(jnp.float32).reshape(shape)
    return (s / cnt).astype(x.dtype)

def pool_mixer(u, pool_w, pool_scale, grid):
    B, L, _ = u.shape
    outs = []
    for gi, w in enumerate(POOL_WINDOWS):
        ug = u[..., gi * POOL_GROUP_DIM:(gi + 1) * POOL_GROUP_DIM]
        if grid:
            rows = L // GRID_W
            ug2 = ug.reshape(B, rows, GRID_W, POOL_GROUP_DIM)
            m = centred_window_mean(centred_window_mean(ug2, w, 1), w, 2)
            m = m.reshape(B, L, POOL_GROUP_DIM)
        else:
            m = centred_window_mean(ug, w, 1)
        outs.append(m - ug)
    p = jnp.stack(outs, axis=2)
    p = jnp.einsum('blgc,gcd->blgd', p, pool_w).reshape(B, L, POOL_DIM)
    return p * pool_scale

def short_conv(x, w):
    C = x.shape[-1]
    return lax.conv_general_dilated(
        x, w[:, None, :].astype(x.dtype), window_strides=(1,),
        padding=[(CONV_K // 2, CONV_K // 2)],
        dimension_numbers=('NWC', 'WIO', 'NWC'), feature_group_count=C)

def gated_delta_chunked(q, k, v, beta, g, s0):
    B, L, H, DK = q.shape
    DV = v.shape[-1]
    n = L // CHUNK

    def blocks(t):
        t = t.astype(jnp.float32).reshape((B, n, CHUNK, H) + t.shape[3:])
        return jnp.moveaxis(t, 3, 1)

    q, k, v, beta, g = blocks(q), blocks(k), blocks(v), blocks(beta), blocks(g)
    g = jnp.cumsum(g, axis=-1)
    strict = jnp.tril(jnp.ones((CHUNK, CHUNK), bool), -1)
    incl = jnp.tril(jnp.ones((CHUNK, CHUNK), bool))
    decay = jnp.exp(jnp.where(incl, g[..., :, None] - g[..., None, :], -jnp.inf))
    k_beta = k * beta[..., None]
    lmat = jnp.where(strict, jnp.einsum('bhnck,bhnsk->bhncs', k_beta, k) * decay, 0.0)
    a = lmat + jnp.eye(CHUNK, dtype=jnp.float32)
    rhs = jnp.concatenate([v * beta[..., None], k_beta * jnp.exp(g)[..., None]], axis=-1)
    sol = lax.linalg.triangular_solve(a, rhs, left_side=True, lower=True, unit_diagonal=True)
    u, w = sol[..., :DV], sol[..., DV:]
    attn = jnp.einsum('bhnck,bhnsk->bhncs', q, k) * decay
    q_dec = q * jnp.exp(g)[..., None]
    k_dec = k * jnp.exp(g[..., -1:] - g)[..., None]
    d_last = jnp.exp(g[..., -1])
    xs = (jnp.moveaxis(u, 2, 0), jnp.moveaxis(w, 2, 0), jnp.moveaxis(q_dec, 2, 0),
          jnp.moveaxis(k_dec, 2, 0), jnp.moveaxis(attn, 2, 0), jnp.moveaxis(d_last, 2, 0))

    def step(S, inp):
        u_c, w_c, q_c, k_c, attn_c, d_c = inp
        v_new = u_c - jnp.einsum('bhck,bhkv->bhcv', w_c, S)
        o_c = (jnp.einsum('bhck,bhkv->bhcv', q_c, S)
               + jnp.einsum('bhcs,bhsv->bhcv', attn_c, v_new))
        S = S * d_c[..., None, None] + jnp.einsum('bhck,bhcv->bhkv', k_c, v_new)
        return S, o_c

    s_final, o = lax.scan(step, s0.astype(jnp.float32), xs)
    o = jnp.transpose(o, (1, 0, 3, 2, 4)).reshape(B, L, H, DV)
    return o, s_final

def deltanet_mixer(proj, conv_w, a_log, dt_bias, onorm_g, s0_f, s0_b):
    B, L, _ = proj.shape
    qkv = jax.nn.silu(short_conv(proj[..., OFF_Q:OFF_G], conv_w)).astype(jnp.float32)
    q = qkv[..., :DN_DIM].reshape(B, L, DN_HEADS, DN_HEAD_DIM)
    k = qkv[..., DN_DIM:2 * DN_DIM].reshape(B, L, DN_HEADS, DN_HEAD_DIM)
    v = qkv[..., 2 * DN_DIM:].reshape(B, L, DN_HEADS, DN_HEAD_DIM)
    q = l2norm(q) * (DN_HEAD_DIM ** -0.5)
    k = l2norm(k)
    gate = proj[..., OFF_G:OFF_BETA].astype(jnp.float32).reshape(B, L, DN_HEADS, DN_HEAD_DIM)
    beta = jax.nn.sigmoid(proj[..., OFF_BETA:OFF_ALPHA].astype(jnp.float32)).reshape(B, L, 2, DN_HEADS)
    a_in = proj[..., OFF_ALPHA:OFF_MERGE].astype(jnp.float32).reshape(B, L, 2, DN_HEADS)
    g = -jnp.exp(a_log.astype(jnp.float32)) * jax.nn.softplus(a_in + dt_bias.astype(jnp.float32))
    o_f, s_f = gated_delta_chunked(q, k, v, beta[:, :, 0], g[:, :, 0], s0_f)
    flip = lambda t: jnp.flip(t, axis=1)
    o_b, s_b = gated_delta_chunked(flip(q), flip(k), flip(v), flip(beta[:, :, 1]),
                                   flip(g[:, :, 1]), s0_b)
    o = o_f + flip(o_b)
    o = o * lax.rsqrt(jnp.mean(o * o, axis=-1, keepdims=True) + EPS)
    o = o * onorm_g.astype(jnp.float32) * jax.nn.silu(gate)
    return o.reshape(B, L, DN_DIM).astype(proj.dtype), s_f, s_b

def expert_choice_ffn(h, router_w, w_gate, w_up, w_down):
    B, N, _ = h.shape
    cap = EC_FACTOR * N // N_EXPERTS
    aff = jax.nn.softmax(jnp.einsum('bnd,de->bne', h, router_w).astype(jnp.float32), axis=-1)
    gates, idx = lax.top_k(jnp.swapaxes(aff, 1, 2), cap)
    bidx = jnp.arange(B)[:, None, None]
    xs = h[bidx, idx]
    hid = (jax.nn.silu(jnp.einsum('becd,edf->becf', xs, w_gate))
           * jnp.einsum('becd,edf->becf', xs, w_up))
    ys = jnp.einsum('becf,efd->becd', hid, w_down) * gates[..., None].astype(h.dtype)
    return jnp.zeros_like(h).at[bidx, idx].add(ys)

def trunk_layer(x, cond, s0_f, s0_b, grid, ada_w, ada_b, norm1_g, norm2_g, w_in, pool_w,
                pool_scale, pool_proj, dn_conv, dn_a_log, dn_dt_bias, dn_onorm_g, dn_proj,
                w_out, router_w, exp_w_gate, exp_w_up, exp_w_down):
    mod = jax.nn.silu(cond) @ ada_w + ada_b
    shift1, scale1, gate1, shift2, scale2, gate2 = jnp.split(mod[:, None, :], 6, axis=-1)
    h = rmsnorm(x, norm1_g) * (1 + scale1) + shift1
    proj = h @ w_in
    a_out = pool_mixer(proj[..., OFF_POOL:OFF_Q], pool_w, pool_scale, grid) @ pool_proj
    b_in, s_f, s_b = deltanet_mixer(proj, dn_conv, dn_a_log, dn_dt_bias, dn_onorm_g, s0_f, s0_b)
    b_out = b_in @ dn_proj
    merge = jax.nn.sigmoid(proj[..., OFF_MERGE:])
    mixed = merge[..., :D_MODEL] * a_out + merge[..., D_MODEL:] * b_out
    x = x + gate1 * (mixed @ w_out)
    h = rmsnorm(x, norm2_g) * (1 + scale2) + shift2
    x = x + gate2 * expert_choice_ffn(h, router_w, exp_w_gate, exp_w_up, exp_w_down)
    return x, s_f, s_b

def setup_inputs(seed: int = 0) -> dict:
    key = jax.random.key(seed)
    ks = jax.random.split(key, 26)
    f32 = jnp.float32

    def nrm(k, shape, scale):
        return jax.random.normal(k, shape, f32) * scale

    st_shape = (DEC_BATCH, DEPTH, DN_HEADS, DN_HEAD_DIM, DN_HEAD_DIM)
    a_log = jnp.log(jax.random.uniform(ks[10], (DEPTH, 2, DN_HEADS), f32, 1.0, 16.0))
    dt = jax.random.uniform(ks[11], (DEPTH, 2, DN_HEADS), f32, 1e-3, 1e-1)
    dt_bias = dt + jnp.log(-jnp.expm1(-dt))
    return {
        "x_prompt": nrm(ks[0], (BATCH, SEQ, D_MODEL), 1.0),
        "x_sample": nrm(ks[1], (DEC_BATCH, DEC_SEQ, D_MODEL), 1.0),
        "state_dn_fwd": nrm(ks[2], st_shape, 0.5),
        "state_dn_bwd": nrm(ks[3], st_shape, 0.5),
        "c": nrm(ks[4], (DEC_BATCH, D_MODEL), 1.0),
        "c_ctx": nrm(ks[5], (D_MODEL,), 1.0),
        "ada_w": nrm(ks[6], (DEPTH, D_MODEL, 6 * D_MODEL), 0.02),
        "ada_b": nrm(ks[7], (DEPTH, 6 * D_MODEL), 0.02),
        "norm1_g": 1.0 + nrm(ks[8], (DEPTH, D_MODEL), 0.05),
        "norm2_g": 1.0 + nrm(ks[9], (DEPTH, D_MODEL), 0.05),
        "w_in": nrm(ks[12], (DEPTH, D_MODEL, IN_COLS), D_MODEL ** -0.5),
        "pool_w": nrm(ks[13], (DEPTH, POOL_GROUPS, POOL_GROUP_DIM, POOL_GROUP_DIM), POOL_GROUP_DIM ** -0.5),
        "pool_scale": 1.0 + nrm(ks[14], (DEPTH, POOL_DIM), 0.1),
        "pool_proj": nrm(ks[15], (DEPTH, POOL_DIM, D_MODEL), POOL_DIM ** -0.5),
        "dn_conv": nrm(ks[16], (DEPTH, CONV_K, 3 * DN_DIM), CONV_K ** -0.5),
        "dn_a_log": a_log,
        "dn_dt_bias": dt_bias,
        "dn_onorm_g": 1.0 + nrm(ks[17], (DEPTH, DN_HEAD_DIM), 0.05),
        "dn_proj": nrm(ks[18], (DEPTH, DN_DIM, D_MODEL), DN_DIM ** -0.5),
        "w_out": nrm(ks[19], (DEPTH, D_MODEL, D_MODEL), D_MODEL ** -0.5),
        "router_w": nrm(ks[20], (DEPTH, D_MODEL, N_EXPERTS), D_MODEL ** -0.5),
        "exp_w_gate": nrm(ks[21], (DEPTH, N_EXPERTS, D_MODEL, EXPERT_DIM), D_MODEL ** -0.5),
        "exp_w_up": nrm(ks[22], (DEPTH, N_EXPERTS, D_MODEL, EXPERT_DIM), D_MODEL ** -0.5),
        "exp_w_down": nrm(ks[23], (DEPTH, N_EXPERTS, EXPERT_DIM, D_MODEL), EXPERT_DIM ** -0.5),
        "final_norm_g": 1.0 + nrm(ks[24], (D_MODEL,), 0.05),
    }

def reference(x_prompt, x_sample, state_dn_fwd, state_dn_bwd, c, c_ctx, ada_w, ada_b,
              norm1_g, norm2_g, w_in, pool_w, pool_scale, pool_proj, dn_conv, dn_a_log,
              dn_dt_bias, dn_onorm_g, dn_proj, w_out, router_w, exp_w_gate, exp_w_up,
              exp_w_down, final_norm_g):
    def run_layer(x, cond, s0_f, s0_b, grid, l):
        return trunk_layer(x, cond, s0_f, s0_b, grid, ada_w[l], ada_b[l], norm1_g[l],
                           norm2_g[l], w_in[l], pool_w[l], pool_scale[l], pool_proj[l],
                           dn_conv[l], dn_a_log[l], dn_dt_bias[l], dn_onorm_g[l], dn_proj[l],
                           w_out[l], router_w[l], exp_w_gate[l], exp_w_up[l], exp_w_down[l])

    B = x_prompt.shape[0]
    zero_state = jnp.zeros((B, DN_HEADS, DN_HEAD_DIM, DN_HEAD_DIM), jnp.float32)
    xp = x_prompt
    fwd_states, bwd_states = [], []
    for l in range(DEPTH):
        xp, s_f, s_b = run_layer(xp, c_ctx[None, :], zero_state, zero_state, False, l)
        fwd_states.append(s_f.astype(x_prompt.dtype))
        bwd_states.append(s_b.astype(x_prompt.dtype))
    y_prompt = rmsnorm(xp, final_norm_g)
    new_state_dn_fwd = jnp.stack(fwd_states, axis=1)
    new_state_dn_bwd = jnp.stack(bwd_states, axis=1)

    xs = x_sample
    for l in range(DEPTH):
        xs, _, _ = run_layer(xs, c, state_dn_fwd[:, l], state_dn_bwd[:, l], True, l)
    y_sample = rmsnorm(xs, final_norm_g)
    return (y_prompt, y_sample, new_state_dn_fwd, new_state_dn_bwd)


_drawn_inputs = setup_inputs


def setup_inputs(seed=0):
    import zlib

    import numpy as np

    out = dict(_drawn_inputs(seed))
    spreads = {}
    factors = {'state_dn_fwd': 6.441,
     'state_dn_bwd': 5.19,
     'norm2_g': 3.198,
     'pool_scale': 2.74,
     'dn_onorm_g': 7.294}
    for name, (base, spread) in spreads.items():
        noise = np.random.default_rng([zlib.crc32(name.encode()), seed]).standard_normal(out[name].shape)
        drawn = base * np.exp(spread * noise) if base else spread * noise
        out[name] = jnp.asarray(drawn.astype(out[name].dtype))
    for name, factor in factors.items():
        out[name] = (out[name] * factor).astype(out[name].dtype)
    return out
```

```python
from contextlib import ExitStack

import numpy as np
import concourse.bass as bass
from concourse import mybir

ALU = mybir.AluOpType
ACT = mybir.ActivationFunctionType
F32 = mybir.dt.float32
F16 = mybir.dt.float16
U32 = mybir.dt.uint32
AX_X = mybir.AxisListType.X

P = 128
D = 1024
KD = D // P
CTX, LAT = 128, 1024
T = CTX + LAT
NT = T // P
H = 8
NG = 4
WINDOWS = (2, 4, 8, 16)
GRID_W = 64
GRID_H = LAT // GRID_W
TAPS = 5
PAD = TAPS // 2
E = 16
CAP_L, CAP_C = 2 * LAT // E, 2 * CTX // E
CAP = CAP_L + CAP_C
EPS = 1e-6
OFF_POOL = 0
OFF_Q = NG * P
OFF_K = OFF_Q + D
OFF_V = OFF_K + D
OFF_G = OFF_V + D
OFF_BETA = OFF_G + D
OFF_ALPHA = OFF_BETA + 2 * H
OFF_MERGE = OFF_ALPHA + 2 * H
IN_COLS = OFF_MERGE + 2 * D
LEVELS = (2, 4, 8, 16, 32, 64)
PW = CTX + LAT + 4 * PAD
CW = PW - 2 * PAD
LAT0 = CTX + 2 * PAD

ROW_ADA_B, ROW_NORM1, ROW_PSCALE, ROW_ONORM, ROW_CCTX, ROW_C = 0, 48, 56, 60, 61, 69
N_ROWS = 77
CONV_ROWS = TAPS * 3 * H

ONCE = {
    "pe": ["cols_T", "mod_rows_T", "bd_filled", "gsum_filled", "gT_filled", "affT_filled", "topkT_filled"],
    "act": ["silu_c_ready", "x_std", "sig_exp", "softplus_ln", "g_exp", "route_exp"],
    "dve": ["cols_ready", "x_rstd", "modT_ready", "mod_rows", "absz", "g_ready", "gc_ready",
            "gT_ready", "halo_zero", "amp2_ready", "route_shift", "aff_ready", "topk_ready", "routes_ready"],
}


def tcol(t):
    return 0 if t == 0 else LAT0 + (t - 1) * P


def build(nc, a, out_p, out_s, out_sf, out_sb, dbg=None, stop=99):
    ctx = ExitStack()
    with ctx:
        sems = {}

        def sem(name):
            if name not in sems:
                sems[name] = ctx.enter_context(nc.semaphore(name))
            return sems[name]

        def reach(step):
            return sem(next(f"{e}_once" for e, steps in ONCE.items() if step in steps)), 1

        def at_step(step):
            e = next(e for e, steps in ONCE.items() if step in steps)
            return sem(f"{e}_once"), ONCE[e].index(step) + 1

        WORDS = (nc.sbuf_usable_end - nc.sbuf_base) // 4 - 64
        arena = ctx.enter_context(nc.sbuf_tensor("arena", [P, WORDS], F32))
        banks = [ctx.enter_context(nc.psum_tensor(f"bank{i}", [P, 512], F32)) for i in range(8)]
        at_word = [0]

        def take(n):
            o = at_word[0]
            at_word[0] += n
            assert at_word[0] <= WORDS, (at_word[0], WORDS)
            return arena[:, o:o + n]

        mod_dram = nc.dram_tensor("mod_dram", (2, 6 * D), F32).ap()
        b_dram = nc.dram_tensor("b_dram", (H * P, T), F32).ap()
        g_dram = nc.dram_tensor("g_dram", (2 * H, T), F32).ap()
        h2_dram = nc.dram_tensor("h2_dram", (T, D), F32).ap()
        x2_dram = nc.dram_tensor("x2_dram", (T, D), F32).ap()

        ident, ones, tri_f, tri_b = (take(P) for _ in range(4))
        ident_h, nident_h = (take(P // 2).bitcast(F16) for _ in range(2))
        mask_words = take(2 * 7 * P)
        masks = mask_words.bitcast(U32).rearrange("p (s l c) -> p s l c", s=2, l=7)
        cols = take(N_ROWS)
        conv_w = take(CONV_ROWS)
        silu_c = take(2 * KD)
        modT = take(2 * 48)
        amp1 = take(2 * KD)
        small = take(32)
        eps_c, qscale_c, one_c = small[:, 0:1], small[:, 1:2], small[:, 2:3]
        tab = {n: take(NT * 2 * H).rearrange("p (t d) -> p t d", t=NT)
               for n in ("beta", "nbeta", "g", "gc", "nbeg", "kd", "dl", "tmp", "tmp2")}
        PERSIST = at_word[0]
        hT = take(KD * T)
        hT3 = hT.rearrange("p (k t) -> p k t", k=KD)
        BT_AT = at_word[0]
        bT = take(KD * T)
        HEADS_AT = at_word[0]

        block = ctx.enter_context(nc.Block())
        progs = {"sync": [], "scalar": [], "vector": [], "gpsimd": [], "tensor": []}

        at_word[0] = BT_AT
        x_all = take(NT * D).rearrange("p (t d) -> p t d", t=NT)
        at_word[0] = HEADS_AT
        ada_slot = [take(KD * D).rearrange("p (k n) -> p k n", k=KD) for _ in range(2)]
        rows_in = take(P)
        convr_in = take(P)
        modr = take(P)

        ada_rows = a["ada_b"].rearrange("l (r p) -> (l r) p", p=P)
        modT3 = modT.rearrange("p (c m) -> p c m", c=2)
        cols2 = cols[:, ROW_CCTX:ROW_CCTX + 16].rearrange("p (c k) -> p c k", c=2)
        silu3 = silu_c.rearrange("p (c k) -> p c k", c=2)
        amp3 = amp1.rearrange("p (c k) -> p c k", c=2)

        def sync1(sp):
            for i, name in enumerate(("ident", "ones", "tri_f", "tri_b")):
                sp.dma_start((ident, ones, tri_f, tri_b)[i], a["consts"][i]).then_inc(sem("consts_in"), 16)
            sp.dma_start(masks, a["masks"].rearrange("s l p c -> p s l c")).then_inc(sem("consts_in"), 16)
            for src, row in ((ada_rows, ROW_ADA_B), (a["norm1_g"].rearrange("l (r p) -> (l r) p", p=P), ROW_NORM1),
                             (a["pool_scale"].rearrange("l (r p) -> (l r) p", p=P), ROW_PSCALE),
                             (a["dn_onorm_g"], ROW_ONORM),
                             (a["c_ctx"].rearrange("(r p) -> r p", p=P), ROW_CCTX),
                             (a["c"].rearrange("b (r p) -> (b r) p", p=P), ROW_C)):
                sp.dma_start(rows_in[row:row + src.shape[0], :], src).then_inc(sem("consts_in"), 16)
            sp.dma_start(convr_in[0:CONV_ROWS, :], a["dn_conv"].rearrange("l t (j p) -> (l t j) p", p=P)).then_inc(sem("consts_in"), 16)
            for g in range(6):
                if g >= 2:
                    sp.wait_ge(sem("ada_used"), g - 1)
                sp.dma_start(ada_slot[g % 2], a["ada_w"][0].rearrange("(k p) n -> p k n", p=P)[:, :, g * D:(g + 1) * D]).then_inc(sem(f"ada_in{g % 2}"), 16)
                if g == 1:
                    sp.dma_start(x_all[:, 0, :], a["x_prompt"][0]).then_inc(sem("x_in"), 16)
                    for t in range(1, NT):
                        sp.dma_start(x_all[:, t, :], a["x_sample"][0, (t - 1) * P:t * P, :]).then_inc(sem("x_in"), 16)

        N_CONSTS = 12 * 16

        def pe1(pe):
            pe.wait_ge(sem("consts_in"), N_CONSTS)
            nc.tensor.transpose(banks[0][:, 0:N_ROWS], rows_in[0:N_ROWS, :], ident[0:N_ROWS, 0:N_ROWS])
            nc.tensor.transpose(banks[0][:, 128:128 + CONV_ROWS], convr_in[0:CONV_ROWS, :], ident[0:CONV_ROWS, 0:CONV_ROWS]).then_inc(*reach("cols_T"))
            pe.wait_ge(*at_step("silu_c_ready"))
            for g in range(6):
                pe.wait_ge(sem(f"ada_in{g % 2}"), 16 * (g // 2 + 1))
                for m in range(KD):
                    for k in range(KD):
                        o = 2 * (g * KD + m)
                        last = nc.tensor.matmul(banks[1][:, o:o + 2], ada_slot[g % 2][:, k, m * P:(m + 1) * P],
                                                silu3[:, :, k], start=(k == 0), stop=(k == KD - 1))
                last.then_inc(sem("ada_used"), 1)
            pe.wait_ge(*at_step("modT_ready"))
            nc.tensor.transpose(banks[0][0:96, 256:384], modT, ident).then_inc(*reach("mod_rows_T"))

        def act1(act):
            act.wait_ge(*at_step("cols_ready"))
            nc.scalar.activation(silu3, cols2, ACT.Silu).then_inc(*reach("silu_c_ready"))
            act.wait_ge(sem("x_in"), 16 * NT)
            for t in range(NT):
                last = nc.scalar.activation(hT[:, t * D:(t + 1) * D] if t < NT - 1 else hT[:, (t - 1) * D:t * D], x_all[:, t, :],
                                            ACT.Square, accum_out=small[:, 8 + t:9 + t])
                last.then_inc(sem("act_order"), 1)
                act.wait_ge(sem("act_order"), t + 1)
            nc.scalar.activation(small[:, 20:20 + NT], small[:, 8:8 + NT], ACT.Sqrt, scale=1.0 / D, bias=eps_c).then_inc(*reach("x_std"))

        def dve1(dve):
            nc.vector.memset(eps_c, EPS)
            nc.vector.memset(qscale_c, -0.5 * float(np.log(P)))
            nc.vector.memset(one_c, 1.0)
            dve.wait_ge(*at_step("cols_T"))
            nc.vector.tensor_copy(cols, banks[0][:, 0:N_ROWS])
            nc.vector.tensor_copy(conv_w, banks[0][:, 128:128 + CONV_ROWS]).then_inc(*reach("cols_ready"))
            dve.wait_ge(*at_step("x_std"))
            nc.vector.reciprocal(small[:, 8:8 + NT], small[:, 20:20 + NT]).then_inc(*reach("x_rstd"))
            dve.wait_ge(*at_step("x_rstd"))
            for t in range(NT):
                nc.vector.tensor_scalar(x_all[:, t, :], x_all[:, t, :], small[:, 8 + t:9 + t], None, ALU.mult).then_inc(sem("xn_ready"), 1)
            dve.wait_ge(sem("ada_used"), 6)
            for c in range(2):
                nc.vector.tensor_tensor(modT3[:, c, :], banks[1][:, 0:96].rearrange("p (m c) -> p c m", c=2)[:, c, :],
                                        cols[:, ROW_ADA_B:ROW_ADA_B + 48], ALU.add).then_inc(sem("dve_mod"), 1)
            dve.wait_ge(sem("dve_mod"), 2)
            for c in range(2):
                last = nc.vector.scalar_tensor_tensor(amp3[:, c, :], modT3[:, c, KD:2 * KD], 1.0,
                                                      cols[:, ROW_NORM1:ROW_NORM1 + KD], ALU.add, ALU.mult)
            last.then_inc(*reach("modT_ready"))
            dve.wait_ge(*at_step("mod_rows_T"))
            nc.vector.tensor_copy(modr[0:96, :], banks[0][0:96, 256:384]).then_inc(*reach("mod_rows"))

        def sync1b(sp):
            sp.wait_ge(*at_step("mod_rows"))
            sp.dma_start(mod_dram.rearrange("c (m p) -> (c m) p", p=P), modr[0:96, :]).then_inc(sem("mod_saved"), 16)

        H_USES = [(0, k, 0) for k in range(KD)] + [(1, k, half) for half in range(2) for k in range(KD)]

        def pe2(pe):
            for j, (c, k, half) in enumerate(H_USES):
                if j >= 6:
                    pe.wait_ge(sem("hT_drained"), j - 5)
                tiles = [0] if c == 0 else [1 + 4 * half + i for i in range(4)]
                pe.wait_ge(sem("xn_ready"), tiles[-1] + 1)
                for i, t in enumerate(tiles):
                    last = nc.tensor.transpose(banks[2 + j % 6][:, i * P:(i + 1) * P], x_all[:, t, k * P:(k + 1) * P], ident)
                last.then_inc(sem("xT_filled"), 1)

        def act2(act):
            act.wait_ge(*at_step("modT_ready"))
            for j, (c, k, half) in enumerate(H_USES):
                act.wait_ge(sem("xT_filled"), j + 1)
                n, at = (CTX, 0) if c == 0 else (512, CTX + 512 * half)
                nc.scalar.activation(hT3[:, k, at:at + n], banks[2 + j % 6][:, 0:n], ACT.Identity,
                                     scale=amp3[:, c, k:k + 1], bias=modT3[:, c, k:k + 1]).then_inc(sem("hT_drained"), 1)

        w_bd = take(KD * 4 * H).rearrange("p (k n) -> p k n", k=KD)
        bias_rows = take(2 * H)
        alog_rows = take(2 * H)
        gT_rows = take(T)
        tokcols = banks[0][:, 0:NT * 32].rearrange("p (t n) -> p t n", t=NT)

        def sync3(sp):
            sp.wait_ge(sem("mod_saved"), 16)
            sp.dma_start(w_bd, a["w_in"][0].rearrange("(k p) n -> p k n", p=P)[:, :, OFF_BETA:OFF_MERGE]).then_inc(sem("bd_in"), 16)
            sp.dma_start(bias_rows, a["dn_dt_bias"].rearrange("l d h -> l (d h)").to_broadcast([P, 2 * H])).then_inc(sem("bd_in"), 16)
            sp.dma_start(alog_rows, a["dn_a_log"].rearrange("l d h -> l (d h)").to_broadcast([P, 2 * H])).then_inc(sem("bd_in"), 16)
            sp.wait_ge(*at_step("gT_ready"))
            sp.dma_start(g_dram, gT_rows[0:2 * H, :]).then_inc(sem("g_saved"), 16)
            sp.wait_ge(sem("g_saved"), 16)

        def pe3(pe):
            pe.wait_ge(sem("bd_in"), 48)
            pe.wait_ge(sem("hT_drained"), len(H_USES))
            for t in range(NT):
                for k in range(KD):
                    last = nc.tensor.matmul(tokcols[:, t, :], hT3[:, k, t * P:(t + 1) * P], w_bd[:, k, :],
                                            start=(k == 0), stop=(k == KD - 1))
            last.then_inc(*reach("bd_filled"))
            pe.wait_ge(*at_step("g_ready"))
            for d, tri in enumerate((tri_f, tri_b)):
                nc.tensor.matmul(banks[2][:, d * NT * H:(d + 1) * NT * H], tri, tab["g"][:, :, d * H:(d + 1) * H], start=True, stop=True)
            nc.tensor.matmul(banks[3][:, 0:NT * 2 * H], ones, tab["g"].rearrange("p t d -> p (t d)"), start=True, stop=True).then_inc(*reach("gsum_filled"))
            pe.wait_ge(*at_step("gc_ready"))
            for t in range(NT):
                last = nc.tensor.transpose(banks[4 + t // 3][0:2 * H, (t % 3) * P:(t % 3 + 1) * P], tab["gc"][:, t, :], ident)
            last.then_inc(*reach("gT_filled"))

        def act3(act):
            act.wait_ge(*at_step("bd_filled"))
            nc.scalar.activation(tab["beta"], tokcols[:, :, 0:2 * H], ACT.Exp, scale=-1.0)
            act.wait_ge(sem("bd_in"), 48)
            nc.scalar.activation(alog_rows, alog_rows, ACT.Exp).then_inc(*reach("sig_exp"))
            act.wait_ge(*at_step("absz"))
            nc.scalar.activation(tab["tmp2"], tab["tmp2"], ACT.Exp, scale=-1.0).then_inc(sem("act_order"), 1)
            act.wait_ge(sem("act_order"), NT + 1)
            nc.scalar.activation(tab["tmp2"], tab["tmp2"], ACT.Ln, bias=one_c).then_inc(*reach("softplus_ln"))
            act.wait_ge(*at_step("gc_ready"))
            nc.scalar.activation(tab["kd"], tab["kd"], ACT.Exp)
            nc.scalar.activation(tab["dl"], tab["tmp"], ACT.Exp)
            nc.scalar.activation(tab["nbeg"], tab["gc"], ACT.Exp).then_inc(*reach("g_exp"))

        def dve3(dve):
            n = [0]

            def step(ins):
                n[0] += 1
                ins.then_inc(sem("dve_decay"), 1)
                dve.wait_ge(sem("dve_decay"), n[0])

            dve.wait_ge(*at_step("sig_exp"))
            step(nc.vector.tensor_scalar(tab["beta"], tab["beta"], 1.0, None, ALU.add))
            step(nc.vector.reciprocal(tab["beta"], tab["beta"]))
            nc.vector.tensor_scalar(tab["nbeta"], tab["beta"], -1.0, None, ALU.mult)
            step(nc.vector.tensor_tensor(tab["tmp"], tokcols[:, :, 2 * H:4 * H], bias_rows.unsqueeze(1).to_broadcast([P, NT, 2 * H]), ALU.add))
            nc.vector.tensor_scalar(tab["tmp2"], tab["tmp"], -1.0, None, ALU.mult).then_inc(sem("dve_decay"), 1)
            n[0] += 1
            dve.wait_ge(sem("dve_decay"), n[0])
            nc.vector.tensor_tensor(tab["tmp2"], tab["tmp2"], tab["tmp"], ALU.max).then_inc(*reach("absz"))
            dve.wait_ge(*at_step("softplus_ln"))
            step(nc.vector.scalar_tensor_tensor(tab["g"], tab["tmp"], 0.0, tab["tmp2"], ALU.max, ALU.add))
            step(nc.vector.tensor_tensor(tab["g"], tab["g"], alog_rows.unsqueeze(1).to_broadcast([P, NT, 2 * H]), ALU.mult))
            nc.vector.tensor_scalar(tab["g"], tab["g"], -1.0, None, ALU.mult).then_inc(*reach("g_ready"))
            dve.wait_ge(*at_step("gsum_filled"))
            nc.vector.tensor_copy(tab["tmp"].rearrange("p t d -> p (t d)"), banks[3][:, 0:NT * 2 * H])
            for d in range(2):
                step(nc.vector.tensor_copy(tab["gc"][:, :, d * H:(d + 1) * H],
                                           banks[2][:, d * NT * H:(d + 1) * NT * H].rearrange("p (t h) -> p t h", h=H)))
            nc.vector.tensor_tensor(tab["kd"], tab["tmp"], tab["gc"], ALU.subtract).then_inc(*reach("gc_ready"))
            dve.wait_ge(*at_step("g_exp"))
            nc.vector.tensor_tensor(tab["nbeg"], tab["nbeg"], tab["nbeta"], ALU.mult)
            dve.wait_ge(*at_step("gT_filled"))
            for b in range(3):
                last = nc.vector.tensor_copy(gT_rows[0:2 * H, b * 384:(b + 1) * 384], banks[4 + b][0:2 * H, 0:384])
            last.then_inc(*reach("gT_ready"))

        at_word[0] = BT_AT
        w_head = [take(KD * P).rearrange("p (k n) -> p k n", k=KD) for _ in range(4)]
        raw = [take(PW) for _ in range(3)]
        qkvg = [take(PW) for _ in range(4)]
        qT, kT, vT, gateT = qkvg
        v3 = lambda x: x.rearrange("p (t c) -> p t c", t=NT)
        half = lambda: v3(take(T // 2).bitcast(F16))
        grow = [take(T) for _ in range(2)]
        dm_flat = [take(T) for _ in range(2)]
        kq_flat = [take(T) for _ in range(2)]
        dm, kq = [v3(x) for x in dm_flat], [v3(x) for x in kq_flat]
        attnT = [v3(take(T)) for _ in range(2)]
        ktok, vtok = v3(take(T)), v3(take(T))
        vb = [v3(take(T)) for _ in range(2)]
        Yf = [v3(take(T)) for _ in range(2)]
        nL, nLlo = [half() for _ in range(2)], [half() for _ in range(2)]
        Xs, Ys, Zs = ([half() for _ in range(2)] for _ in range(3))
        S = [[take(P) for _ in range(2)] for _ in range(2)]
        scan = vT[:, 0:6 * P].rearrange("p (s d c) -> p s d c", s=3, d=2)
        orow = small[:, 8:8 + NT]
        TRI = (banks[0:3], banks[3:6])
        USES = {0: ["nq", "kT", "kk"], 1: ["nk", "vT", "kq"]}
        for d in range(2):
            USES[d] += ["LT", "Y2"]
            for b in LEVELS:
                USES[d] += [f"Z{b}", f"P{b}", f"X{b}"]
            USES[d] += ["res", "fix"]
        USES[0] += ["oT"]
        BY_DVE = {(d, n) for d in range(2) for n in ["vT", "LT", "oT", "fix"] + [f"P{b}" for b in LEVELS]}
        BY_DVE |= {(1, "res")} | {(1, f"Z{b}") for b in LEVELS}

        def use(d, name):
            return USES[d].index(name)

        def filled(eng, h, d, name, g):
            eng.wait_ge(sem(f"filled{d}"), h * (3 * len(USES[d])) + 3 * use(d, name) + g + 1)

        def drained_sem(d, name):
            return sem(f"drained{d}_{'dve' if (d, name) in BY_DVE else 'act'}")

        def drained_count(h, d, name, g):
            mine = [n for n in USES[d] if ((d, n) in BY_DVE) == ((d, name) in BY_DVE)]
            return h * (3 * len(mine)) + 3 * mine.index(name) + g + 1

        def drained(eng, h, d, name, g):
            before = USES[d][use(d, name) - 1]
            eng.wait_ge(drained_sem(d, before), drained_count(h, d, before, g))

        def all_drained(eng, h, d, name):
            eng.wait_ge(drained_sem(d, name), drained_count(h, d, name, 2))

        def alone(eng):
            eng.sem_inc(sem("waits_kept"), 1)

        def tile_at(d, t):
            return t if d == 0 or t == 0 else NT - t

        SPAN = ((0, CTX), (CTX, 512), (CTX + 512, 512))
        UNITS = 12
        MATS = (3, 0, 1, 2)

        def unit_count(h, u):
            return UNITS * (h + 1) + u - 2

        def project(pe, h, i0, i1):
            for i in range(i0, i1):
                u, k = i // KD, i % KD
                at, n = SPAN[u % 3]
                m = MATS[u // 3]
                if k == 0:
                    if u % 3 == 0:
                        pe.wait_ge(sem(f"w_in{m}"), 16 * (h + 1 if m == 3 else h + 2))
                    if not (isinstance(h, int) and h == -1 and u < 5):
                        pe.wait_ge(sem("pj_drained"), unit_count(h, u) - 2)
                ins = nc.tensor.matmul(banks[6 + u % 2][:, 0:n], w_head[m][:, k, :], hT3[:, k, at:at + n], start=(k == 0), stop=(k == KD - 1))
                if k == KD - 1:
                    ins.then_inc(sem("pj_filled"), 1)

        SPANS_RAW = (PAD, LAT0 + PAD, LAT0 + PAD + 512)
        SPANS_CONV = (0, LAT0, LAT0 + 512)

        def evac_unit(act, h, u):
            n = SPAN[u % 3][1]
            act.wait_ge(sem("pj_filled"), unit_count(h, u))
            if u < 3:
                dst = gateT[:, SPANS_CONV[u]:SPANS_CONV[u] + n]
            else:
                at = SPANS_RAW[u % 3]
                dst = raw[u // 3 - 1][:, at:at + n]
            nc.scalar.activation(dst, banks[6 + u % 2][:, 0:n], ACT.Copy).then_inc(sem("pj_drained"), 1)

        def load_w(sp, h, j):
            off = (OFF_Q, OFF_K, OFF_V, OFF_G)[j]
            sp.dma_start(w_head[j], a["w_in"][0].rearrange("(k p) n -> p k n", p=P)[:, :, bass.ds(off + h * P, P)]).then_inc(sem(f"w_in{j}"), 16)

        def load_decay_and_state(sp, h):
            for d in range(2):
                sp.dma_start(grow[d], g_dram[bass.ds(h + d * H, 1), :].to_broadcast([P, T])).then_inc(sem(f"grow_in{d}"), 16)
                sp.dma_start(S[d][1], (a["state_dn_fwd"], a["state_dn_bwd"])[d].rearrange("b l h k v -> (b l h k) v")[bass.ds(h * P, P), :]).then_inc(sem(f"S_in{d}"), 16)

        def store_states(sp, h):
            for d in range(2):
                sp.wait_ge(sem(f"S_upd{d}"), h * (NT + 1) + 2)
                sp.dma_start((out_sf, out_sb)[d].rearrange("b l h k v -> (b l h k) v")[bass.ds(h * P, P), :], S[d][0]).then_inc(sem(f"S_out{d}"), 16)

        def store_b(sp, h):
            sp.wait_ge(sem("b_ready"), h + 1)
            sp.dma_start(b_dram[bass.ds(h * P, P), :], kq_flat[1]).then_inc(sem("b_out"), 16)

        def sync4(sp):
            sp.wait_ge(sem("scan_done"), 1)
            sp.dma_start(small[0:1, 29:32], a["consts"][0][0:1, 0:3]).then_inc(sem("b_out"), 16)
            for j in range(4):
                load_w(sp, 0, j)
            load_decay_and_state(sp, 0)
            with sp.Fori(0, H - 1) as h:
                sp.wait_ge(sem("pj_filled"), unit_count(h - 1, UNITS - 1))
                for j in range(3):
                    load_w(sp, h + 1, j)
                sp.wait_ge(sem("pj_filled"), unit_count(h, 2))
                load_w(sp, h + 1, 3)
                store_states(sp, h)
                store_b(sp, h)
                sp.wait_ge(sem("scan_done"), h + 2)
                load_decay_and_state(sp, h + 1)
            store_states(sp, H - 1)
            store_b(sp, H - 1)

        def body_pe(pe, h, last_h=False):
            fill = (lambda *x: None) if last_h else (lambda i0, i1: project(pe, h, i0, i1))
            project(pe, h, 0, 3 * KD)
            pe.wait_ge(sem("scan_done"), h + 1)
            for d, name in enumerate(("nq", "nk")):
                pe.wait_ge(sem("sq_ready"), 2 * h + d + 1)
                for b, (at, n) in enumerate(SPAN):
                    nc.tensor.matmul(TRI[d][b][:, 0:n], ones, dm_flat[d][:, at:at + n], start=True, stop=True).then_inc(sem(f"filled{d}"), 1)
                fill(*((24, 32), (32, 40))[d])
            for d, name in ((1, "vT"), (0, "kT")):
                pe.wait_ge(sem("k_normed" if d == 0 else "v_ready"), h + 1)
                for g in range(3):
                    drained(pe, h, d, name, g)
                    for i in range(3):
                        last = nc.tensor.transpose(TRI[d][g][:, i * P:(i + 1) * P], (kT, vT)[d][:, tcol(3 * g + i):tcol(3 * g + i) + P], ident)
                    last.then_inc(sem(f"filled{d}"), 1)
            pe.wait_ge(sem("q_normed"), h + 1)
            for d, name in enumerate(("kk", "kq")):
                for g in range(3):
                    drained(pe, h, d, name, g)
                    for i in range(3):
                        at = tcol(3 * g + i)
                        last = nc.tensor.matmul(TRI[d][g][:, i * P:(i + 1) * P], kT[:, at:at + P], (kT, qT)[d][:, at:at + P], start=True, stop=True)
                    last.then_inc(sem(f"filled{d}"), 1)
            fill(40, 48)
            for d in range(2):
                for g in range(3):
                    pe.wait_ge(sem("lt_ready"), 6 * h + 3 * d + g + 1)
                    drained(pe, h, d, "LT", g)
                    for i in range(3):
                        last = nc.tensor.transpose(TRI[d][g][:, i * P:(i + 1) * P], Yf[d][:, 3 * g + i, :], ident)
                    last.then_inc(sem(f"filled{d}"), 1)

            def turn(d, name, src):
                for g in range(3):
                    drained(pe, h, d, name, g)
                    for i in range(3):
                        last = nc.tensor.transpose(TRI[d][g].bitcast(F16)[:, i * P:(i + 1) * P], src[d][:, 3 * g + i, :], ident_h)
                    last.then_inc(sem(f"filled{d}"), 1)

            def products(d, name, terms):
                for g in range(3):
                    drained(pe, h, d, name, g)
                    for i in range(3):
                        for n, (lhs, rhs) in enumerate(terms):
                            last = nc.tensor.matmul(TRI[d][g][:, i * P:(i + 1) * P], lhs if lhs.shape[1] == P else lhs[:, 3 * g + i, :],
                                                    rhs if rhs.shape[1] == P else rhs[:, 3 * g + i, :],
                                                    start=(n == 0), stop=(n == len(terms) - 1))
                    last.then_inc(sem(f"filled{d}"), 1)

            for d in range(2):
                pe.wait_ge(sem("X_init"), 6 * h + 3 * d + 3)
                turn(d, "Y2", Xs)
            for lv, b in enumerate(LEVELS):
                for d in range(2):
                    products(d, f"Z{b}", [(nL[d], Ys[d])])
                fill(48 + 4 * lv, 50 + 4 * lv)
                for d in range(2):
                    products(d, f"P{b}", [(Xs[d], Zs[d])])
                fill(50 + 4 * lv, 52 + 4 * lv)
                for d in range(2):
                    turn(d, f"X{b}", Ys)
            for d in range(2):
                pe.wait_ge(sem("nLlo_ready"), 2 * h + d + 1)
                products(d, "res", [(nL[d], Ys[d]), (nLlo[d], Ys[d]), (nident_h, Ys[d]), (ident_h, ident_h)])
            for d in range(2):
                products(d, "fix", [(Xs[d], Zs[d])])
            for d in range(2):
                all_drained(pe, h, d, "fix")
                pe.wait_ge(sem("qd_ready"), 2 * h + d + 1)
                pe.wait_ge(sem("attn_ready"), 2 * h + d + 1)
            slot = 9 * KD
            for t in range(NT):
                for d in range(2):
                    s, ti = S[d][min(t, 1)], tile_at(d, t)
                    at = tcol(ti)
                    pe.wait_ge(sem(f"S_upd{d}"), h * (NT + 1) + t + 1)
                    if t == 1:
                        pe.wait_ge(sem(f"S_in{d}"), 16 * h + 16)
                    nc.tensor.matmul(TRI[d][0][:, 0:P], kT[:, at:at + P], s, start=True, stop=True).then_inc(sem(f"kS_filled{d}"), 1)
                fill(slot, min(slot + 1, 96))
                slot = min(slot + 1, 96)
                for d in range(2):
                    pe.wait_ge(sem(f"R_ready{d}"), h * NT + t + 1)
                    nc.tensor.matmul(TRI[d][1][:, 0:P], Yf[d][:, tile_at(d, t), :], scan[:, 0, d, :], start=True, stop=True).then_inc(sem(f"vn_filled{d}"), 1)
                fill(slot, min(slot + 1, 96))
                slot = min(slot + 1, 96)
                for d in range(2):
                    s, ti = S[d][min(t, 1)], tile_at(d, t)
                    pe.wait_ge(sem(f"vn_ready{d}"), h * NT + t + 1)
                    nc.tensor.matmul(TRI[d][0][:, 0:P], ktok[:, ti, :], scan[:, 2, d, :], start=True, stop=True)
                    if t > 0:
                        pe.wait_ge(sem(f"o_drained{d}"), h * NT + t)
                    nc.tensor.matmul(TRI[d][2][:, 0:P], grow[d][:, ti * P:(ti + 1) * P], s, start=True, stop=False)
                    nc.tensor.matmul(TRI[d][2][:, 0:P], attnT[d][:, ti, :], scan[:, 1, d, :], start=False, stop=True).then_inc(sem(f"o_filled{d}"), 1)
                fill(slot, min(slot + 1, 96))
                slot = min(slot + 1, 96)
            pe.wait_ge(sem("o_normed"), h + 1)
            for g in range(3):
                for i in range(3):
                    last = nc.tensor.transpose(TRI[0][g][:, i * P:(i + 1) * P], kq[0][:, 3 * g + i, :], ident)
                last.then_inc(sem("filled0"), 1)

        def flat(x, g):
            return x[:, 3 * g:3 * g + 3, :].rearrange("p t c -> p (t c)")

        def body_act(act, h, last_h=False):
            evac = (lambda u: None) if last_h else (lambda u: evac_unit(act, h, u))

            def silu(j):
                if j < 3:
                    act.wait_ge(sem("conv_done"), 3 * h + j + 1)
                else:
                    act.wait_ge(sem("pj_drained"), unit_count(h, 2))
                for n, at in ((CTX, 0), (LAT, LAT0)):
                    last = nc.scalar.activation(qkvg[j][:, at:at + n], qkvg[j][:, at:at + n], ACT.Silu)
                if j == 2:
                    last.then_inc(sem("v_ready"), 1)
                elif j == 3:
                    last.then_inc(sem("gate_ready"), 1)
                else:
                    last.then_inc(sem("qk_silu"), 1)
                    act.wait_ge(sem("qk_silu"), 2 * h + j + 1)
                    nc.scalar.activation(dm_flat[j][:, 0:CTX], qkvg[j][:, 0:CTX], ACT.Square)
                    nc.scalar.activation(dm_flat[j][:, CTX:T], qkvg[j][:, LAT0:LAT0 + LAT], ACT.Square).then_inc(sem("sq_ready"), 1)

            act.wait_ge(sem("scan_done"), h + 1)
            evac_unit(act, h, 0)
            silu(0)
            evac_unit(act, h, 1)
            silu(1)
            evac_unit(act, h, 2)
            silu(2)
            silu(3)
            evac(3)
            for d in range(2):
                for b, (at, n) in enumerate(SPAN):
                    filled(act, h, d, ("nq", "nk")[d], b)
                    nc.scalar.activation(dm_flat[d][:, at:at + n], TRI[d][b][:, 0:n], ACT.Ln, bias=eps_c).then_inc(sem(f"drained{d}_act"), 1)
                all_drained(act, h, d, ("nq", "nk")[d])
                nc.scalar.activation(dm_flat[d], dm_flat[d], ACT.Exp, scale=-0.5, bias=qscale_c if d == 0 else 0.0).then_inc(sem("rnorm"), 1)
            evac(4)
            for g in range(3):
                filled(act, h, 0, "kT", g)
                nc.scalar.activation(flat(ktok, g), TRI[0][g][:, 0:384], ACT.Copy).then_inc(sem("drained0_act"), 1)
            act.wait_ge(sem("b_out"), 16 * h + 16)
            for d in range(2):
                for g in range(3):
                    filled(act, h, d, ("kk", "kq")[d], g)
                    nc.scalar.activation(kq_flat[d][:, g * 384:(g + 1) * 384], TRI[d][g][:, 0:384], ACT.Copy).then_inc(sem(f"drained{d}_act"), 1)
            for d in range(2):
                act.wait_ge(sem("gdiff"), 2 * h + d + 1)
                nc.scalar.activation(dm_flat[d], dm_flat[d], ACT.Exp).then_inc(sem("decay_exp"), 1)
            for d in range(2):
                nc.scalar.activation(grow[d], grow[d], ACT.Exp).then_inc(sem("grow_exp"), 1)
            evac(5)
            for d in range(2):
                for g in range(3):
                    act.wait_ge(sem("nl_masked"), 6 * h + 3 * d + g + 1)
                    nc.scalar.activation(flat(nL[d], g), flat(Yf[d], g), ACT.Copy).then_inc(sem("nL_ready"), 1)

            def copy(d, name, dst, dt=F32):
                for g in range(3):
                    filled(act, h, d, name, g)
                    src = TRI[d][g] if dt == F32 else TRI[d][g].bitcast(dt)
                    nc.scalar.activation(flat(dst[d], g), src[:, 0:384], ACT.Copy).then_inc(sem(f"drained{d}_act"), 1)

            for d in range(2):
                copy(d, "Y2", Ys, F16)
            for lv, b in enumerate(LEVELS):
                copy(0, f"Z{b}", Zs)
                for d in range(2):
                    copy(d, f"X{b}", Xs, F16)
                if lv % 2 == 1:
                    evac(6 + lv // 2)
            copy(0, "res", Zs)
            for t in range(NT):
                for d in range(2):
                    ti = tile_at(d, t)
                    act.wait_ge(sem(f"vn_filled{d}"), h * NT + t + 1)
                    nc.scalar.activation(scan[:, 2, d, :], TRI[d][1][:, 0:P], ACT.Copy, scale=tab["kd"][:, ti, bass.ds(h + d * H, 1)])
                    nc.scalar.activation(scan[:, 1, d, :], TRI[d][1][:, 0:P], ACT.Copy).then_inc(sem(f"vn_ready{d}"), 1)
                for d in range(2):
                    act.wait_ge(sem(f"o_filled{d}"), h * NT + t + 1)
                    nc.scalar.activation(kq[d][:, tile_at(d, t), :], TRI[d][2][:, 0:P], ACT.Copy).then_inc(sem(f"o_drained{d}"), 1)
                if t in (3, 5, 8):
                    evac({3: 9, 5: 10, 8: 11}[t])
            act.wait_ge(sem("o_sumsq"), h + 1)
            nc.scalar.activation(orow, orow, ACT.Ln, scale=1.0 / P, bias=eps_c).then_inc(sem("o_ln"), 1)
            act.wait_ge(sem("o_ln"), h + 1)
            nc.scalar.activation(orow, orow, ACT.Exp, scale=-0.5).then_inc(sem("o_rstd"), 1)

        def body_dve(dve, h):
            for j in range(3):
                dve.wait_ge(sem("pj_drained"), unit_count(h - 1, 3 * j + 5))
                for tap in range(TAPS):
                    w = conv_w[:, bass.ds(tap * 3 * H + j * H + h, 1)]
                    if tap == 0:
                        ins = nc.vector.tensor_scalar(qkvg[j][:, 0:CW], raw[j][:, 0:CW], w, None, ALU.mult)
                    else:
                        ins = nc.vector.scalar_tensor_tensor(qkvg[j][:, 0:CW], raw[j][:, tap:tap + CW], w, qkvg[j][:, 0:CW], ALU.mult, ALU.add)
                    if tap < TAPS - 1:
                        ins.then_inc(sem("tap_done"), 1)
                        dve.wait_ge(sem("tap_done"), h * (3 * (TAPS - 1)) + j * (TAPS - 1) + tap + 1)
                    else:
                        ins.then_inc(sem("conv_done"), 1)
            for d, name in ((0, "q_normed"), (1, "k_normed")):
                dve.wait_ge(sem("rnorm"), 2 * h + d + 1)
                nc.vector.tensor_tensor(qkvg[d][:, 0:CTX], qkvg[d][:, 0:CTX], dm_flat[d][:, 0:CTX], ALU.mult)
                nc.vector.tensor_tensor(qkvg[d][:, LAT0:LAT0 + LAT], qkvg[d][:, LAT0:LAT0 + LAT], dm_flat[d][:, CTX:T], ALU.mult).then_inc(sem(name), 1)
            for d in range(2):
                dve.wait_ge(sem(f"grow_in{d}"), 16 * h + 16)
                dve.wait_ge(sem("q_normed" if d == 0 else "k_normed"), h + 1)
                for t in range(NT):
                    last = nc.vector.tensor_scalar(dm_flat[d][:, t * P:(t + 1) * P], grow[d][:, t * P:(t + 1) * P],
                                                   tab["gc"][:, t, bass.ds(h + d * H, 1)], 0.0, ALU.subtract, ALU.min)
                last.then_inc(sem("gdiff"), 1)
            for g in range(3):
                filled(dve, h, 1, "vT", g)
                nc.vector.tensor_copy(flat(vtok, g), TRI[1][g][:, 0:384]).then_inc(sem("drained1_dve"), 1)
            for d in range(2):
                dve.wait_ge(sem("decay_masked"), 2 * h + d + 1)
                all_drained(dve, h, 0, "kk")
                for g in range(3):
                    nc.vector.tensor_tensor(Yf[d][:, 3 * g:3 * g + 3, :], kq[0][:, 3 * g:3 * g + 3, :], dm[d][:, 3 * g:3 * g + 3, :], ALU.mult).then_inc(sem("lt_ready"), 1)
            for d in range(2):
                nc.vector.tensor_copy(Xs[d], ident_h.unsqueeze(1).to_broadcast([P, NT, P])).then_inc(sem("X_eye"), 1)
            for d in range(2):
                for g in range(3):
                    filled(dve, h, d, "LT", g)
                    nc.vector.tensor_tensor(Yf[d][:, 3 * g:3 * g + 3, :], TRI[d][g][:, 0:384].rearrange("p (t c) -> p t c", t=3),
                                            tab["nbeta"][:, 3 * g:3 * g + 3, bass.ds(h + d * H, 1)].to_broadcast([P, 3, P]), ALU.mult).then_inc(sem(f"drained{d}_dve"), 1)
            for d in range(2):
                dve.wait_ge(sem("grow_exp"), 2 * h + d + 1)
                nc.vector.tensor_tensor(grow[d][:, 0:CTX], qT[:, 0:CTX], grow[d][:, 0:CTX], ALU.mult)
                nc.vector.tensor_tensor(grow[d][:, CTX:T], qT[:, LAT0:LAT0 + LAT], grow[d][:, CTX:T], ALU.mult).then_inc(sem("qd_ready"), 1)
            dve.wait_ge(sem("X_eye"), 2 * h + 2)
            for d in range(2):
                for g in range(3):
                    dve.wait_ge(sem("nL_ready"), 6 * h + 3 * d + g + 1)
                    alone(dve)
                    nc.vector.copy_predicated(Xs[d][:, 3 * g:3 * g + 3, :], masks[:, d, 0, :].unsqueeze(1).to_broadcast([P, 3, P]), nL[d][:, 3 * g:3 * g + 3, :]).then_inc(sem("X_init"), 1)

            def copy1(name):
                for g in range(3):
                    filled(dve, h, 1, name, g)
                    nc.vector.tensor_copy(flat(Zs[1], g), TRI[1][g][:, 0:384]).then_inc(sem("drained1_dve"), 1)

            for lv, b in enumerate(LEVELS):
                copy1(f"Z{b}")
                for d in range(2):
                    for g in range(3):
                        filled(dve, h, d, f"P{b}", g)
                        alone(dve)
                        nc.vector.copy_predicated(Ys[d][:, 3 * g:3 * g + 3, :], masks[:, 1 - d, lv + 1, :].unsqueeze(1).to_broadcast([P, 3, P]),
                                                  TRI[d][g][:, 0:384].rearrange("p (t c) -> p t c", t=3)).then_inc(sem(f"drained{d}_dve"), 1)
            copy1("res")
            for d in range(2):
                for g in range(3):
                    filled(dve, h, d, "fix", g)
                    nc.vector.tensor_tensor(flat(Yf[d], g), TRI[d][g][:, 0:384], flat(Ys[d], g), ALU.add).then_inc(sem(f"drained{d}_dve"), 1)
            for d in range(2):
                dve.wait_ge(sem("vb_ready"), 2 * h + d + 1)
            for t in range(NT):
                for d in range(2):
                    ti = tile_at(d, t)
                    dve.wait_ge(sem(f"kS_filled{d}"), h * NT + t + 1)
                    nc.vector.scalar_tensor_tensor(scan[:, 0, d, :], TRI[d][0][:, 0:P], tab["nbeg"][:, ti, bass.ds(h + d * H, 1)],
                                                   vb[d][:, ti, :], ALU.mult, ALU.add).then_inc(sem(f"R_ready{d}"), 1)
                for d in range(2):
                    ti = tile_at(d, t)
                    s = S[d][min(t, 1)]
                    dve.wait_ge(sem(f"o_filled{d}"), h * NT + t + 1)
                    nc.vector.scalar_tensor_tensor(s, s, tab["dl"][:, ti, bass.ds(h + d * H, 1)], TRI[d][0][:, 0:P], ALU.mult, ALU.add).then_inc(sem(f"S_upd{d}"), 1)
            dve.wait_ge(sem("o_squared"), h + 1)
            nc.vector.tensor_reduce(orow, kq[1], AX_X, ALU.add).then_inc(sem("o_sumsq"), 1)
            dve.wait_ge(sem("o_rstd"), h + 1)
            nc.vector.tensor_tensor(kq[0], kq[0], orow.unsqueeze(2).to_broadcast([P, NT, P]), ALU.mult).then_inc(sem("o_normed"), 1)
            on = cols[:, ROW_ONORM:ROW_ONORM + 1]
            dve.wait_ge(sem("gate_ready"), h + 1)
            for g in range(3):
                filled(dve, h, 0, "oT", g)
                if g == 0:
                    nc.vector.scalar_tensor_tensor(kq_flat[1][:, 0:P], TRI[0][0][:, 0:P], on, gateT[:, 0:P], ALU.mult, ALU.mult)
                    nc.vector.scalar_tensor_tensor(kq_flat[1][:, P:3 * P], TRI[0][0][:, P:3 * P], on, gateT[:, LAT0:LAT0 + 2 * P], ALU.mult, ALU.mult).then_inc(sem("drained0_dve"), 1)
                else:
                    at = tcol(3 * g)
                    nc.vector.scalar_tensor_tensor(kq_flat[1][:, 3 * g * P:(3 * g + 3) * P], TRI[0][g][:, 0:3 * P], on, gateT[:, at:at + 3 * P], ALU.mult, ALU.mult).then_inc(sem("drained0_dve"), 1)
            nc.vector.memset(small[:, 5:6], 0.0).then_inc(sem("b_ready"), 1)
            nc.vector.memset(small[:, 3:4], 0.0).then_inc(sem("scan_done"), 1)
            for d in range(2):
                dve.wait_ge(sem(f"S_out{d}"), 16 * h + 16)
                nc.vector.memset(S[d][0], 0.0).then_inc(sem(f"S_upd{d}"), 1)

        def dve4_first(dve):
            dve.wait_ge(sem("hT_drained"), len(H_USES))
            dve.wait_ge(sem("g_saved"), 16)
            nc.vector.tensor_copy(ident_h, ident)
            nc.vector.tensor_scalar(nident_h, ident, -1.0, None, ALU.mult)
            for r in raw:
                nc.vector.memset(r[:, 0:PAD], 0.0)
                nc.vector.memset(r[:, PAD + CTX:LAT0 + PAD], 0.0)
                nc.vector.memset(r[:, PW - PAD:PW], 0.0)
            nc.vector.memset(small[:, 3:4], 0.0).then_inc(sem("scan_done"), 1)
            dve.wait_ge(sem("scan_done"), 1)
            for d in range(2):
                nc.vector.memset(S[d][0], 0.0).then_inc(sem(f"S_upd{d}"), 1)

        def body_pool(pool, h):
            for d in range(2):
                sgn = 1 - 2 * d
                pool.wait_ge(sem("decay_exp"), 2 * h + d + 1)
                alone(pool)
                nc.gpsimd.affine_select(out=dm[d], in_=dm[d], compare_op=ALU.is_ge, fill=0.0, base=0,
                                        pattern=[[0, NT], [sgn, P]], channel_multiplier=-sgn).then_inc(sem("decay_masked"), 1)
            for d in range(2):
                for g in range(3):
                    pool.wait_ge(drained_sem(d, "LT"), drained_count(h, d, "LT", g))
                    alone(pool)
                    nc.gpsimd.affine_select(out=Yf[d][:, 3 * g:3 * g + 3, :], in_=Yf[d][:, 3 * g:3 * g + 3, :], compare_op=ALU.not_equal, fill=0.0, base=0,
                                            pattern=[[0, 3], [-1, P]], channel_multiplier=1).then_inc(sem("nl_masked"), 1)
            for d in range(2):
                pool.wait_ge(sem("decay_masked"), 2 * h + d + 1)
                all_drained(pool, h, 1, "kq")
                nc.gpsimd.tensor_tensor(attnT[d], kq[1], dm[d], ALU.mult).then_inc(sem("attn_ready"), 1)
            for d in range(2):
                pool.wait_ge(sem("nL_ready"), 6 * h + 3 * d + 3)
                nc.gpsimd.tensor_tensor(nLlo[d], Yf[d], nL[d], ALU.subtract).then_inc(sem("nLlo_ready"), 1)
            for d in range(2):
                all_drained(pool, h, 1, "vT")
                nc.gpsimd.tensor_tensor(vb[d], vtok, tab["beta"][:, :, bass.ds(h + d * H, 1)].to_broadcast([P, NT, P]), ALU.mult).then_inc(sem("vb_ready"), 1)
            for d in range(2):
                pool.wait_ge(sem(f"o_drained{d}"), (h + 1) * NT)
            nc.gpsimd.tensor_tensor(kq[0], kq[0], kq[1], ALU.add).then_inc(sem("o_added"), 1)
            pool.wait_ge(sem("o_added"), h + 1)
            nc.gpsimd.tensor_tensor(kq[1], kq[0], kq[0], ALU.mult).then_inc(sem("o_squared"), 1)

        def prologue_pe(pe):
            pe.wait_ge(sem("scan_done"), 1)
            project(pe, -1, 3 * KD, 12 * KD)

        def prologue_act(act):
            act.wait_ge(sem("scan_done"), 1)
            for u in range(3, UNITS):
                evac_unit(act, -1, u)

        RES = dict(locals())
        from_later = later(nc, a, RES, out_p, out_s, dbg, stop)

        @block.sync
        def _(sp):
            sync1(sp)
            sync1b(sp)
            sync3(sp)
            if stop >= 4:
                sync4(sp)
            from_later["sync"](sp)

        @block.tensor
        def _(pe):
            pe1(pe)
            pe2(pe)
            pe3(pe)
            if stop >= 4:
                prologue_pe(pe)
                with pe.Fori(0, H - 1) as h:
                    body_pe(pe, h)
                body_pe(pe, H - 1, True)
            from_later["tensor"](pe)

        @block.scalar
        def _(act):
            act1(act)
            act2(act)
            act3(act)
            if stop >= 4:
                prologue_act(act)
                with act.Fori(0, H - 1) as h:
                    body_act(act, h)
                body_act(act, H - 1, True)
            from_later["scalar"](act)

        @block.vector
        def _(dve):
            dve1(dve)
            dve3(dve)
            dve4_first(dve)
            if stop >= 4:
                with dve.Fori(0, H) as h:
                    body_dve(dve, h)
            from_later["vector"](dve)

        @block.gpsimd
        def _(pool):
            if stop >= 4:
                with pool.Fori(0, H) as h:
                    body_pool(pool, h)
            from_later["gpsimd"](pool)


def later(nc, a, v, out_p, out_s, dbg, stop):
    alone, reach, at_step = v["alone"], v["reach"], v["at_step"]
    sem, take, at_word, banks, arena = v["sem"], v["take"], v["at_word"], v["banks"], v["arena"]
    ident, cols, modT3, small, eps_c = v["ident"], v["cols"], v["modT3"], v["small"], v["eps_c"]
    hT3, bT = v["hT3"], v["bT"]
    bT3 = bT.rearrange("p (k t) -> p k t", k=KD)
    HEADS_AT, BT_AT, PERSIST = v["HEADS_AT"], v["BT_AT"], v["PERSIST"]
    mod_dram, h2_dram, x2_dram = v["mod_dram"], v["h2_dram"], v["x2_dram"]
    w_in3 = a["w_in"][0].rearrange("(k p) n -> p k n", p=P)
    COLS = ((0, CTX), (CTX, 512), (CTX + 512, 512))

    at_word[0] = HEADS_AT
    p4 = take(NG * T).rearrange("p (g t) -> p g t", g=NG)
    MIX_AT = at_word[0]
    w_pool = take(KD * NG * P).rearrange("p (k n) -> p k n", k=KD)
    pool_w = take(NG * P).rearrange("p (g n) -> p g n", g=NG)
    inv = take(T)
    u = take(T)
    HALO = WINDOWS[-1] // 2
    GWP, GHP = GRID_W + 2 * HALO, GRID_H + 2 * HALO
    colbuf = [take(GRID_H * GWP).rearrange("p (r c) -> p r c", r=GRID_H) for _ in range(3)]
    rowbuf = [take(GHP * GRID_W).rearrange("p (r c) -> p r c", r=GHP) for _ in range(3)]
    ctxbuf = [take(CTX + 2 * HALO) for _ in range(3)]
    mean = take(T)

    def sync5(sp):
        sp.wait_ge(sem("scan_done"), H + 1)
        sp.wait_ge(sem("b_out"), 16 * H + 16)
        sp.dma_start(bT3, v["b_dram"].rearrange("(k p) t -> p k t", p=P)).then_inc(sem("b_in"), 16)
        for src, dst in ((w_in3[:, :, OFF_POOL:OFF_POOL + NG * P], w_pool), (a["pool_w"][0].rearrange("g c n -> c g n"), pool_w)):
            sp.dma_start(dst, src).then_inc(sem("pool_w_in"), 16)
        for g in range(NG):
            if g > 0:
                sp.wait_ge(sem("pool_in_ready"), g)
            sp.dma_start(inv, a["inv_count"][g:g + 1, :].to_broadcast([P, T])).then_inc(sem("inv_in"), 16)

    def pe5(pe):
        pe.wait_ge(sem("pool_w_in"), 32)
        for g in range(NG):
            if g > 0:
                pe.wait_ge(sem("u_drained"), g)
            else:
                pe.wait_ge(sem("scan_done"), H + 1)
            for b, (at, n) in enumerate(COLS):
                for k in range(KD):
                    last = nc.tensor.matmul(banks[b][:, 0:n], w_pool[:, k, g * P:(g + 1) * P], hT3[:, k, at:at + n], start=(k == 0), stop=(k == KD - 1))
            last.then_inc(sem("u_filled"), 1)
            pe.wait_ge(sem("pool_in_ready"), g + 1)
            if g > 0:
                pe.wait_ge(sem("p4_drained"), g)
            for b, (at, n) in enumerate(COLS):
                last = nc.tensor.matmul(banks[3 + b][:, 0:n], pool_w[:, g, :], mean[:, at:at + n], start=True, stop=True)
            last.then_inc(sem("p4_filled"), 1)

    def act5(act):
        act.wait_ge(*at_step("halo_zero"))
        for g in range(NG):
            act.wait_ge(sem("u_filled"), g + 1)
            if g > 0:
                act.wait_ge(sem("pool_in_ready"), g)
            for b, (at, n) in enumerate(COLS):
                nc.scalar.activation(u[:, at:at + n], banks[b][:, 0:n], ACT.Copy)
            nc.scalar.activation(ctxbuf[0][:, HALO:HALO + CTX], banks[0][:, 0:CTX], ACT.Copy)
            for b in range(2):
                last = nc.scalar.activation(colbuf[0][:, 8 * b:8 * b + 8, HALO:HALO + GRID_W], banks[1 + b][:, 0:512].rearrange("p (r c) -> p r c", c=GRID_W), ACT.Copy)
            last.then_inc(sem("u_drained"), 1)
            act.wait_ge(sem("p4_filled"), g + 1)
            for b, (at, n) in enumerate(COLS):
                last = nc.scalar.activation(p4[:, g, at:at + n], banks[3 + b][:, 0:n], ACT.Copy, scale=cols[:, ROW_PSCALE + g:ROW_PSCALE + g + 1])
            last.then_inc(sem("p4_drained"), 1)

    def dve5(dve):
        n = [0]

        def step(ins):
            n[0] += 1
            ins.then_inc(sem("dve_pool"), 1)
            dve.wait_ge(sem("dve_pool"), n[0])

        nc.vector.memset(colbuf[0], 0.0)
        nc.vector.memset(rowbuf[0], 0.0)
        nc.vector.memset(ctxbuf[0], 0.0).then_inc(*reach("halo_zero"))
        for g, w in enumerate(WINDOWS):
            dve.wait_ge(sem("u_drained"), g + 1)
            m = w.bit_length() - 1
            src, width = colbuf[0], GWP
            for s in range(m):
                sh = 1 << s
                width -= sh
                if s == m - 1:
                    f = HALO - w // 2
                    step(nc.vector.tensor_tensor(rowbuf[0][:, HALO:HALO + GRID_H, :], src[:, :, f:f + GRID_W], src[:, :, f + sh:f + sh + GRID_W], ALU.add))
                else:
                    dst = colbuf[1 + s % 2]
                    step(nc.vector.tensor_tensor(dst[:, :, 0:width], src[:, :, 0:width], src[:, :, sh:sh + width], ALU.add))
                    src = dst
            src, rows = rowbuf[0], GHP
            for s in range(m):
                sh = 1 << s
                rows -= sh
                if s == m - 1:
                    f = HALO - w // 2
                    step(nc.vector.tensor_tensor(mean[:, CTX:T].rearrange("p (r c) -> p r c", c=GRID_W), src[:, f:f + GRID_H, :], src[:, f + sh:f + sh + GRID_H, :], ALU.add))
                else:
                    dst = rowbuf[1 + s % 2]
                    step(nc.vector.tensor_tensor(dst[:, 0:rows, :], src[:, 0:rows, :], src[:, sh:sh + rows, :], ALU.add))
                    src = dst
            src, width = ctxbuf[0], CTX + 2 * HALO
            for s in range(m):
                sh = 1 << s
                width -= sh
                if s == m - 1:
                    f = HALO - w // 2
                    step(nc.vector.tensor_tensor(mean[:, 0:CTX], src[:, f:f + CTX], src[:, f + sh:f + sh + CTX], ALU.add))
                else:
                    dst = ctxbuf[1 + s % 2]
                    step(nc.vector.tensor_tensor(dst[:, 0:width], src[:, 0:width], src[:, sh:sh + width], ALU.add))
                    src = dst
            dve.wait_ge(sem("inv_in"), 16 * (g + 1))
            step(nc.vector.tensor_tensor(mean, mean, inv, ALU.mult))
            nc.vector.tensor_tensor(mean, mean, u, ALU.subtract).then_inc(sem("pool_in_ready"), 1)
            dve.wait_ge(sem("p4_filled"), g + 1)

    at_word[0] = MIX_AT
    mixT = take(KD * T)
    mixT3 = mixT.rearrange("p (k t) -> p k t", k=KD)
    w_outs = take(KD * D).rearrange("p (k n) -> p k n", k=KD)
    KB = 2 * KD + NG + KD
    w_mix = [take(KB * P).rearrange("p (k n) -> p k n", k=KB) for _ in range(2)]
    NTC = 3
    CH = T // NTC
    sg_all = v["mask_words"][:, 0:4 * CH].rearrange("p (s b c) -> p s b c", s=2, b=2)
    sg = [[sg_all[:, i, j, :] for j in range(2)] for i in range(2)]
    BR = ((0, KD), (KD, 2 * KD), (2 * KD, 2 * KD + NG), (2 * KD + NG, KB))

    def load_mix(sp, dt, s):
        for k0, src, col in ((0, w_in3, OFF_MERGE), (KD, w_in3, OFF_MERGE + D),
                             (2 * KD, a["pool_proj"][0].rearrange("(k p) n -> p k n", p=P), 0),
                             (2 * KD + NG, a["dn_proj"][0].rearrange("(k p) n -> p k n", p=P), 0)):
            nk = NG if k0 == 2 * KD else KD
            sp.dma_start(w_mix[s][:, k0:k0 + nk, :], src[:, :, bass.ds(dt * P + col, P)]).then_inc(sem(f"w_mix_in{s}"), 16)

    def sync6(sp):
        sp.wait_ge(sem("p4_drained"), NG)
        for s in range(2):
            load_mix(sp, s, s)
        with sp.Fori(0, KD // 2 - 1) as i:
            for s in range(2):
                sp.wait_ge(sem("mix_filled"), i * (2 * NTC) + (s + 1) * NTC)
                load_mix(sp, i * 2 + 2 + s, s)
        sp.dma_start(w_outs, a["w_out"][0].rearrange("(k p) n -> p k n", p=P)).then_inc(sem("w_out_in"), 16)

    def pe6(pe):
        srcs = (hT3, hT3, p4, bT3)
        pe.wait_ge(sem("b_in"), 16)
        pe.wait_ge(sem("p4_drained"), NG)
        with pe.Fori(0, KD // 2) as i:
            for s in range(2):
                pe.wait_ge(sem(f"w_mix_in{s}"), 64 * i + 64)
                for c in range(NTC):
                    n = s * NTC + c
                    st = n % 2
                    pe.wait_ge(sem("mix_drained"), i * (2 * NTC) + n + 1)
                    for br, (k0, k1) in enumerate(BR):
                        for k in range(k0, k1):
                            last = nc.tensor.matmul(banks[4 * st + br][:, 0:CH], w_mix[s][:, k, :], srcs[br][:, k - k0, c * CH:(c + 1) * CH], start=(k == k0), stop=(k == k1 - 1))
                    last.then_inc(sem("mix_filled"), 1)

    def act6(act):
        with act.Fori(0, KD // 2) as i:
            for n in range(2 * NTC):
                st = n % 2
                act.wait_ge(sem("mix_filled"), i * (2 * NTC) + n + 1)
                act.wait_ge(sem("mix_drained"), i * (2 * NTC) + n + 1)
                for br in range(2):
                    last = nc.scalar.activation(sg[st][br], banks[4 * st + br][:, 0:CH], ACT.Sigmoid)
                last.then_inc(sem("gates_ready"), 1)

    def dve6(dve):
        dve.wait_ge(sem("p4_drained"), NG)
        dve.sem_inc(sem("mix_drained"), 2)
        with dve.Fori(0, KD // 2) as i:
            for n in range(2 * NTC):
                st, s, c = n % 2, n // NTC, n % NTC
                dve.wait_ge(sem("gates_ready"), i * (2 * NTC) + n + 1)
                for br in range(2):
                    nc.vector.tensor_tensor(sg[st][br], sg[st][br], banks[4 * st + 2 + br][:, 0:CH], ALU.mult).then_inc(sem("mix_prod"), 1)
                dve.wait_ge(sem("mix_prod"), i * (4 * NTC) + 2 * n + 2)
                nc.vector.tensor_tensor(mixT[:, bass.ds((i * 2 + s) * T + c * CH, CH)], sg[st][0], sg[st][1], ALU.add).then_inc(sem("mix_drained"), 1)

    at_word[0] = PERSIST
    row = {n: [take(D) for _ in range(2)] for n in ("gate1", "amp2", "shift2")}
    norm2_row = take(D)
    router = take(KD * E).rearrange("p (k e) -> p k e", k=KD)
    assert at_word[0] <= BT_AT
    at_word[0] = BT_AT
    XR = 2
    x_t = [take(D) for _ in range(XR)]
    h2_t = [take(D) for _ in range(XR)]
    prod = [take(D) for _ in range(XR)]
    h2T = [take(D).rearrange("p (k t) -> p k t", k=KD) for _ in range(XR)]
    assert at_word[0] <= HEADS_AT
    st7 = small[:, 5:8]
    ssum = [small[:, 8 + i:9 + i] for i in range(2)]
    rstd = [small[:, 10 + i:11 + i] for i in range(2)]
    lnb = [small[:, 12 + i:13 + i] for i in range(2)]

    def x_tile(t):
        return a["x_prompt"][0] if t == 0 else a["x_sample"][0, (t - 1) * P:t * P, :]

    MIX_ALL = 2 * NTC * (KD // 2) + 2

    def sync7(sp):
        sp.wait_ge(sem("mix_drained"), MIX_ALL)
        for c in range(2):
            for i, n in ((2, "gate1"), (4, "amp2"), (3, "shift2")):
                sp.dma_start(row[n][c], mod_dram[c:c + 1, i * D:(i + 1) * D].to_broadcast([P, D])).then_inc(sem("rows_in"), 16)
        sp.dma_start(norm2_row, a["norm2_g"].to_broadcast([P, D])).then_inc(sem("rows_in"), 16)
        sp.dma_start(router, a["router_w"][0].rearrange("(k p) e -> p k e", p=P)).then_inc(sem("router_in"), 16)
        for t in range(XR):
            sp.dma_start(x_t[t % XR], x_tile(t)).then_inc(sem(f"xt_in{t % XR}"), 16)
        for t in range(NT):
            sp.wait_ge(sem("x1_ready"), t + 1)
            sp.dma_start(x2_dram[t * P:(t + 1) * P, :], x_t[t % XR]).then_inc(sem(f"x1_out{t % XR}"), 16)
            sp.wait_ge(sem("h2_ready"), t + 1)
            sp.dma_start(h2_dram[t * P:(t + 1) * P, :], h2_t[t % XR]).then_inc(sem(f"h2_out{t % XR}"), 16)
            if t + XR < NT:
                sp.wait_ge(sem(f"x1_out{t % XR}"), 16 * (t // XR + 1))
                sp.dma_start(x_t[t % XR], x_tile(t + XR)).then_inc(sem(f"xt_in{t % XR}"), 16)

    def pe7(pe):
        pe.wait_ge(sem("w_out_in"), 16)
        pe.wait_ge(sem("mix_drained"), MIX_ALL)

        def project(t):
            if t >= 2:
                pe.wait_ge(sem("y_drained"), t - 1)
            for half in range(2):
                for k in range(KD):
                    last = nc.tensor.matmul(banks[2 * (t % 2) + half][:, 0:512], mixT3[:, k, t * P:(t + 1) * P], w_outs[:, k, half * 512:(half + 1) * 512], start=(k == 0), stop=(k == KD - 1))
            last.then_inc(sem("y_filled"), 1)

        project(0)
        pe.wait_ge(sem("router_in"), 16)
        for t in range(NT):
            if t + 1 < NT:
                project(t + 1)
            pe.wait_ge(sem("h2_ready"), t + 1)
            if t > 0:
                pe.wait_ge(sem("h2T_ready"), t)
            for k in range(KD):
                last = nc.tensor.transpose(banks[4 + k // 4][:, (k % 4) * P:(k % 4 + 1) * P], h2_t[t % XR][:, k * P:(k + 1) * P], ident)
            last.then_inc(sem("h2T_filled"), 1)
            pe.wait_ge(sem("h2T_ready"), t + 1)
            for k in range(KD):
                last = nc.tensor.matmul(banks[6][:, t * E:(t + 1) * E], h2T[t % XR][:, k, :], router[:, k, :], start=(k == 0), stop=(k == KD - 1))
            last.then_inc(sem("logits_filled"), 1)

    def act7(act):
        for t in range(NT):
            act.wait_ge(sem("x1_ready"), t + 1)
            nc.scalar.activation(prod[t % XR], x_t[t % XR], ACT.Square, accum_out=ssum[t % 2]).then_inc(sem("act7"), 1)
            act.wait_ge(sem("act7"), 2 * t + 1)
            nc.scalar.activation(lnb[t % 2], ssum[t % 2], ACT.Ln, scale=1.0 / D, bias=eps_c).then_inc(sem("act7"), 1)
            act.wait_ge(sem("act7"), 2 * t + 2)
            nc.scalar.activation(rstd[t % 2], lnb[t % 2], ACT.Exp, scale=-0.5).then_inc(sem("rstd2"), 1)
            act.wait_ge(sem("h2T_filled"), t + 1)
            for i in range(2):
                last = nc.scalar.activation(h2T[t % XR][:, 4 * i:4 * i + 4, :].rearrange("p k t -> p (k t)"), banks[4 + i][:, 0:512], ACT.Copy)
            last.then_inc(sem("h2T_ready"), 1)

    def dve7(dve):
        dve.wait_ge(sem("rows_in"), 16 * 7)
        for c in range(2):
            last = nc.vector.scalar_tensor_tensor(row["amp2"][c], row["amp2"][c], 1.0, norm2_row, ALU.add, ALU.mult)
        last.then_inc(*reach("amp2_ready"))
        dve.wait_ge(*at_step("amp2_ready"))
        for t in range(NT):
            c, s = min(t, 1), t % XR
            dve.wait_ge(sem("y_filled"), t + 1)
            if t >= 2:
                dve.wait_ge(sem("rstd2"), t - 1)
            for half in range(2):
                last = nc.vector.tensor_tensor(prod[s][:, half * 512:(half + 1) * 512], banks[2 * (t % 2) + half][:, 0:512], row["gate1"][c][:, half * 512:(half + 1) * 512], ALU.mult)
            last.then_inc(sem("y_drained"), 1)
            dve.wait_ge(sem("y_drained"), t + 1)
            dve.wait_ge(sem(f"xt_in{s}"), 16 * (t // XR + 1))
            nc.vector.tensor_tensor(x_t[s], x_t[s], prod[s], ALU.add).then_inc(sem("x1_ready"), 1)
            dve.wait_ge(sem("rstd2"), t + 1)
            if t >= XR:
                dve.wait_ge(sem(f"h2_out{s}"), 16 * (t // XR))
                dve.wait_ge(sem("h2T_filled"), t - 1)
            nc.vector.scalar_tensor_tensor(h2_t[s], x_t[s], rstd[t % 2], row["amp2"][c], ALU.mult, ALU.mult).then_inc(sem("h2_scaled"), 1)
            dve.wait_ge(sem("h2_scaled"), t + 1)
            nc.vector.tensor_tensor(h2_t[s], h2_t[s], row["shift2"][c], ALU.add).then_inc(sem("h2_ready"), 1)

    at_word[0] = PERSIST
    routing = {n: take(NT * E) for n in ("logit", "aff")}
    mx, sm = take(NT), take(NT)
    affT = take(T)
    work = take(T)
    vals, idxu, idxf = take(CAP), take(CAP).bitcast(U32), take(CAP)
    gates_l, gates_c, idx_l, idx_c = take(E), take(E), take(E).bitcast(U32), take(E).bitcast(U32)
    idx_now = [take(4).bitcast(U32) for _ in range(2)]
    ROUTE_END = at_word[0]
    lg3 = routing["logit"].rearrange("p (t e) -> p t e", t=NT)
    af3 = routing["aff"].rearrange("p (t e) -> p t e", t=NT)

    def dve8(dve):
        n = [0]

        def step(ins):
            n[0] += 1
            ins.then_inc(sem("dve_route"), 1)
            dve.wait_ge(sem("dve_route"), n[0])

        dve.wait_ge(sem("logits_filled"), NT)
        lps = banks[6][:, 0:NT * E].rearrange("p (t e) -> p t e", t=NT)
        step(nc.vector.tensor_reduce(mx, lps, AX_X, ALU.max))
        nc.vector.tensor_tensor(lg3, lps, mx.unsqueeze(2).to_broadcast([P, NT, E]), ALU.subtract).then_inc(*reach("route_shift"))
        dve.wait_ge(*at_step("route_exp"))
        step(nc.vector.tensor_reduce(sm, af3, AX_X, ALU.add))
        step(nc.vector.reciprocal(sm, sm))
        nc.vector.tensor_tensor(af3, af3, sm.unsqueeze(2).to_broadcast([P, NT, E]), ALU.mult).then_inc(*reach("aff_ready"))
        dve.wait_ge(*at_step("affT_filled"))
        for b in range(3):
            last = nc.vector.tensor_copy(affT[0:E, b * 384:(b + 1) * 384], banks[b][0:E, 0:384])
        step(last)
        for at, n_tok, cap, col in ((CTX, LAT, CAP_L, 0), (0, CTX, CAP_C, CAP_L)):
            row_ = affT[0:E, at:at + n_tok]
            for r in range(cap // 8):
                o = col + 8 * r
                step(nc.vector.max(vals[0:E, o:o + 8], row_))
                step(nc.vector.max_index(idxu[0:E, o:o + 8], vals[0:E, o:o + 8], row_))
                if r < cap // 8 - 1:
                    step(nc.vector.match_replace(row_, vals[0:E, o:o + 8], row_, -1.0))
        step(nc.vector.tensor_copy(idxf[0:E, :], idxu[0:E, :]))
        nc.vector.tensor_scalar(idxf[0:E, 0:CAP_L], idxf[0:E, 0:CAP_L], float(CTX), None, ALU.add).then_inc(*reach("topk_ready"))
        dve.wait_ge(*at_step("topkT_filled"))
        nc.vector.tensor_copy(gates_l, banks[3][:, 0:E])
        nc.vector.tensor_copy(gates_c[0:CAP_C, :], banks[3][0:CAP_C, E:2 * E])
        nc.vector.tensor_copy(idx_l, banks[3][:, 2 * E:3 * E])
        nc.vector.tensor_copy(idx_c[0:CAP_C, :], banks[3][0:CAP_C, 3 * E:4 * E]).then_inc(*reach("routes_ready"))

    def act8(act):
        act.wait_ge(*at_step("route_shift"))
        nc.scalar.activation(routing["aff"], routing["logit"], ACT.Exp).then_inc(*reach("route_exp"))

    def pe8(pe):
        pe.wait_ge(*at_step("aff_ready"))
        for t in range(NT):
            last = nc.tensor.transpose(banks[t // 3][0:E, (t % 3) * P:(t % 3 + 1) * P], af3[:, t, :], ident)
        last.then_inc(*reach("affT_filled"))
        pe.wait_ge(*at_step("topk_ready"))
        nc.tensor.transpose(banks[3][:, 0:E], vals[0:E, 0:CAP_L], ident[0:E, 0:E])
        nc.tensor.transpose(banks[3][0:CAP_C, E:2 * E], vals[0:E, CAP_L:CAP], ident[0:E, 0:E])
        nc.tensor.transpose(banks[3][:, 2 * E:3 * E], idxf[0:E, 0:CAP_L], ident[0:E, 0:E])
        nc.tensor.transpose(banks[3][0:CAP_C, 3 * E:4 * E], idxf[0:E, CAP_L:CAP], ident[0:E, 0:E]).then_inc(*reach("topkT_filled"))

    NU = 6
    HALF = D // 2
    w_unit = [take(KD * HALF).rearrange("p (k n) -> p k n", k=KD) for _ in range(NU)]
    xs_l, xs_c = take(D), take(D)
    xsT = take(KD * CAP).rearrange("p (k c) -> p k c", k=KD)
    hid = take(KD * CAP).rearrange("p (k c) -> p k c", k=KD)
    sil = [take(CAP) for _ in range(2)]
    ysT = take(KD * CAP).rearrange("p (k c) -> p k c", k=KD)
    ys_l, ys_c = take(D), take(D)
    WMATS = ((0, 0), (1, 0), (0, 1), (1, 1), (2, 0), (2, 1))

    def load_unit(sp, e, u_):
        m, half = WMATS[u_]
        src = a[("exp_w_gate", "exp_w_up", "exp_w_down")[m]][0].rearrange("e k n -> (e k) n")[bass.ds(e * D, D), half * HALF:(half + 1) * HALF]
        sp.dma_start(w_unit[u_], src.rearrange("(k p) n -> p k n", p=P)).then_inc(sem(f"unit_in{u_}"), 16)

    def sync9(sp):
        sp.wait_ge(sem("logits_filled"), NT)
        for s in range(XR):
            n_s = len(range(s, NT, XR))
            sp.wait_ge(sem(f"x1_out{s}"), 16 * n_s)
            sp.wait_ge(sem(f"h2_out{s}"), 16 * n_s)
        for u_ in range(NU):
            load_unit(sp, 0, u_)
        with sp.Fori(0, E - 1) as e:
            for name, units in (("gu_filled", (0, 1, 2, 3)), ("dn_filled", (4, 5))):
                for u_ in units:
                    half = WMATS[u_][1]
                    sp.wait_ge(sem(name), e * KD + (half + 1) * (KD // 2))
                    load_unit(sp, e + 1, u_)

    def gather(pool, e):
        pool.wait_ge(sem("gather_idx"), e + 1)
        alone(pool)
        nc.gpsimd.indirect_dma_start(xs_l, None, h2_dram, bass.IndirectOffsetOnAxis(ap=idx_now[0][:, 0:1], axis=0)).then_inc(sem("xs_in"), 16)
        nc.gpsimd.indirect_dma_start(xs_c[0:CAP_C, :], None, h2_dram, bass.IndirectOffsetOnAxis(ap=idx_now[0][0:CAP_C, 1:2], axis=0)).then_inc(sem("xs_in"), 16)

    def scatter(pool, e):
        pool.wait_ge(sem("ys_ready"), e + 1)
        alone(pool)
        nc.gpsimd.indirect_dma_start(x2_dram, bass.IndirectOffsetOnAxis(ap=idx_now[1][:, 0:1], axis=0), ys_l, None, compute_op=ALU.add).then_inc(sem("scattered"), 16)
        nc.gpsimd.indirect_dma_start(x2_dram, bass.IndirectOffsetOnAxis(ap=idx_now[1][0:CAP_C, 1:2], axis=0), ys_c[0:CAP_C, :], None, compute_op=ALU.add).then_inc(sem("scattered"), 16)
        pool.wait_ge(sem("scattered"), e * 32 + 32)
        alone(pool)
        nc.gpsimd.memset(small[:, 3:4], 0.0).then_inc(sem("scatter_free"), 1)

    def pool9(pool):
        for s in range(XR):
            n_s = len(range(s, NT, XR))
            pool.wait_ge(sem(f"x1_out{s}"), 16 * n_s)
            pool.wait_ge(sem(f"h2_out{s}"), 16 * n_s)
        pool.sem_inc(sem("scatter_free"), 1)
        gather(pool, 0)
        with pool.Fori(0, E - 1) as e:
            gather(pool, e + 1)
            scatter(pool, e)
        scatter(pool, E - 1)

    def body9_pe(pe, e):
        pe.wait_ge(sem("xs_in"), 32 * e + 32)
        pe.wait_ge(sem("ysT_drained"), e + 1)
        for k in range(KD):
            o = (k % 3) * CAP
            nc.tensor.transpose(banks[k // 3][:, o:o + CAP_L], xs_l[:, k * P:(k + 1) * P], ident)
            last = nc.tensor.transpose(banks[k // 3][:, o + CAP_L:o + CAP], xs_c[0:CAP_C, k * P:(k + 1) * P], ident[0:CAP_C, 0:CAP_C])
        last.then_inc(sem("xsT_filled"), 1)
        pe.wait_ge(sem("xsT_ready"), e + 1)
        for f in range(KD):
            half, col = f // 4, (f % 4) * P
            if f % 4 == 0:
                pe.wait_ge(sem(f"unit_in{2 * half}"), 16 * e + 16)
                pe.wait_ge(sem(f"unit_in{2 * half + 1}"), 16 * e + 16)
            pe.wait_ge(sem("gu_drained"), e * KD + f + 1)
            for m in range(2):
                for k in range(KD):
                    last = nc.tensor.matmul(banks[3 + f % 2][:, m * CAP:(m + 1) * CAP], w_unit[2 * half + m][:, k, col:col + P], xsT[:, k, :], start=(k == 0), stop=(k == KD - 1))
            last.then_inc(sem("gu_filled"), 1)
        for dt in range(KD):
            half, col = dt // 4, (dt % 4) * P
            if dt == 0:
                pe.wait_ge(sem("gu_drained"), e * KD + KD + 2)
            if dt % 4 == 0:
                pe.wait_ge(sem(f"unit_in{4 + half}"), 16 * e + 16)
            pe.wait_ge(sem("dn_drained"), e * KD + dt + 1)
            for k in range(KD):
                last = nc.tensor.matmul(banks[5 + dt % 2][:, 0:CAP], w_unit[4 + half][:, k, col:col + P], hid[:, k, :], start=(k == 0), stop=(k == KD - 1))
            last.then_inc(sem("dn_filled"), 1)
        pe.wait_ge(sem("dn_drained"), e * KD + KD + 2)
        for dt in range(KD):
            o = (dt % 4) * P
            nc.tensor.transpose(banks[dt // 4][:, o:o + P], ysT[:, dt, 0:CAP_L], ident)
            last = nc.tensor.transpose(banks[(2, 7)[dt // 4]][0:CAP_C, o:o + P], ysT[:, dt, CAP_L:CAP], ident)
        last.then_inc(sem("ysT_filled"), 1)

    def body9_act(act, e):
        act.wait_ge(sem("xsT_filled"), e + 1)
        for b, nk in ((0, 3), (1, 3), (2, 2)):
            last = nc.scalar.activation(xsT[:, 3 * b:3 * b + nk, :].rearrange("p k c -> p (k c)"), banks[b][:, 0:nk * CAP], ACT.Copy)
        last.then_inc(sem("xsT_ready"), 1)
        for f in range(KD):
            act.wait_ge(sem("gu_filled"), e * KD + f + 1)
            nc.scalar.activation(sil[f % 2], banks[3 + f % 2][:, 0:CAP], ACT.Silu).then_inc(sem("sil_ready"), 1)
        for dt in range(KD):
            act.wait_ge(sem("dn_filled"), e * KD + dt + 1)
            nc.scalar.activation(ysT[:, dt, 0:CAP_L], banks[5 + dt % 2][:, 0:CAP_L], ACT.Copy, scale=modT3[:, 1, 5 * KD + dt:5 * KD + dt + 1])
            nc.scalar.activation(ysT[:, dt, CAP_L:CAP], banks[5 + dt % 2][:, CAP_L:CAP], ACT.Copy, scale=modT3[:, 0, 5 * KD + dt:5 * KD + dt + 1]).then_inc(sem("dn_drained"), 1)

    def set_gather_idx(e):
        nc.vector.tensor_copy(idx_now[0][:, 0:1], idx_l[:, bass.ds(e, 1)])
        nc.vector.tensor_copy(idx_now[0][0:CAP_C, 1:2], idx_c[0:CAP_C, bass.ds(e, 1)]).then_inc(sem("gather_idx"), 1)

    def dve9_first(dve):
        for name, k in (("gu_drained", 2), ("dn_drained", 2), ("ysT_drained", 1)):
            dve.sem_inc(sem(name), k)
        dve.wait_ge(*at_step("routes_ready"))
        set_gather_idx(0)

    def body9_dve(dve, e, last_e=False):
        for f in range(KD):
            dve.wait_ge(sem("sil_ready"), e * KD + f + 1)
            nc.vector.tensor_tensor(hid[:, f, :], sil[f % 2], banks[3 + f % 2][:, CAP:2 * CAP], ALU.mult).then_inc(sem("gu_drained"), 1)
        if not last_e:
            dve.wait_ge(sem("xs_in"), 32 * e + 32)
            set_gather_idx(e + 1)
        dve.wait_ge(sem("ysT_filled"), e + 1)
        dve.wait_ge(sem("scatter_free"), e + 1)
        nc.vector.tensor_copy(idx_now[1][:, 0:1], idx_l[:, bass.ds(e, 1)])
        nc.vector.tensor_copy(idx_now[1][0:CAP_C, 1:2], idx_c[0:CAP_C, bass.ds(e, 1)])
        for half in range(2):
            nc.vector.tensor_scalar(ys_l[:, half * 512:(half + 1) * 512], banks[half][:, 0:512], gates_l[:, bass.ds(e, 1)], None, ALU.mult)
        for half in range(2):
            last = nc.vector.tensor_scalar(ys_c[0:CAP_C, half * 512:(half + 1) * 512], banks[(2, 7)[half]][0:CAP_C, 0:512], gates_c[0:CAP_C, bass.ds(e, 1)], None, ALU.mult)
        last.then_inc(sem("ys_ready"), 1)
        nc.vector.memset(small[:, 4:5], 0.0).then_inc(sem("ysT_drained"), 1)

    at_word[0] = ROUTE_END
    fin_row = take(D)
    xf = [take(D) for _ in range(3)]
    yf = [take(D) for _ in range(3)]
    sqf = take(D)
    fss, fln, frs = take(NT), take(NT), take(NT)

    def sync10(sp):
        sp.wait_ge(sem("scattered"), 32 * E)
        sp.dma_start(fin_row, a["final_norm_g"].rearrange("(o d) -> o d", o=1).to_broadcast([P, D])).then_inc(sem("fin_in"), 16)
        for t in range(NT):
            if t >= 3:
                sp.wait_ge(sem("yf_ready"), t - 2)
            sp.dma_start(xf[t % 3], x2_dram[t * P:(t + 1) * P, :]).then_inc(sem(f"xf_in{t % 3}"), 16)
            if t >= 2:
                store_y(sp, t - 2)
        store_y(sp, NT - 2)
        store_y(sp, NT - 1)
        for s in range(3):
            sp.wait_ge(sem(f"y_out{s}"), 16 * 3)
        for d in range(2):
            sp.wait_ge(sem(f"S_out{d}"), 16 * H)

    def store_y(sp, t):
        dst = out_p[0] if t == 0 else out_s[0, (t - 1) * P:t * P, :]
        sp.wait_ge(sem("yf_ready"), t + 1)
        sp.dma_start(dst, yf[t % 3]).then_inc(sem(f"y_out{t % 3}"), 16)

    def act10(act):
        for t in range(NT):
            act.wait_ge(sem(f"xf_in{t % 3}"), 16 * (t // 3 + 1))
            nc.scalar.activation(sqf, xf[t % 3], ACT.Square, accum_out=fss[:, t:t + 1]).then_inc(sem("act10"), 1)
            act.wait_ge(sem("act10"), 2 * t + 1)
            nc.scalar.activation(fln[:, t:t + 1], fss[:, t:t + 1], ACT.Ln, scale=1.0 / D, bias=eps_c).then_inc(sem("act10"), 1)
            act.wait_ge(sem("act10"), 2 * t + 2)
            nc.scalar.activation(frs[:, t:t + 1], fln[:, t:t + 1], ACT.Exp, scale=-0.5).then_inc(sem("frs_ready"), 1)

    def dve10(dve):
        dve.wait_ge(sem("fin_in"), 16)
        for t in range(NT):
            dve.wait_ge(sem("frs_ready"), t + 1)
            if t >= 3:
                dve.wait_ge(sem(f"y_out{t % 3}"), 16 * (t // 3))
            nc.vector.scalar_tensor_tensor(yf[t % 3], xf[t % 3], frs[:, t:t + 1], fin_row, ALU.mult, ALU.mult).then_inc(sem("yf_ready"), 1)

    def f_sync(sp):
        if stop >= 5:
            sync5(sp)
        if stop >= 6:
            sync6(sp)
            sync7(sp)
        if stop >= 9:
            sync9(sp)
            sync10(sp)

    def f_pe(pe):
        if stop >= 5:
            pe5(pe)
        if stop >= 6:
            pe6(pe)
            pe7(pe)
        if stop >= 8:
            pe8(pe)
        if stop >= 9:
            with pe.Fori(0, E) as e:
                body9_pe(pe, e)

    def f_act(act):
        if stop >= 5:
            act5(act)
        if stop >= 6:
            act6(act)
            act7(act)
        if stop >= 8:
            act8(act)
        if stop >= 9:
            with act.Fori(0, E) as e:
                body9_act(act, e)
            act10(act)

    def f_dve(dve):
        if stop >= 5:
            dve5(dve)
        if stop >= 6:
            dve6(dve)
            dve7(dve)
        if stop >= 8:
            dve8(dve)
        if stop >= 9:
            dve9_first(dve)
            with dve.Fori(0, E - 1) as e:
                body9_dve(dve, e)
            body9_dve(dve, E - 1, True)
            dve10(dve)

    def f_pool(pool):
        if stop >= 9:
            pool9(pool)

    return {"sync": f_sync, "tensor": f_pe, "scalar": f_act, "vector": f_dve, "gpsimd": f_pool, **{"bT": bT}}


_INS = ["x_prompt", "x_sample", "state_dn_fwd", "state_dn_bwd", "c", "c_ctx", "ada_w", "ada_b", "norm1_g",
        "norm2_g", "w_in", "pool_w", "pool_scale", "pool_proj", "dn_conv", "dn_a_log", "dn_dt_bias",
        "dn_onorm_g", "dn_proj", "w_out", "router_w", "exp_w_gate", "exp_w_up", "exp_w_down", "final_norm_g"]
_OUTS = [(1, CTX, D), (1, LAT, D), (1, 1, H, P, P), (1, 1, H, P, P)]


def shape_constants():
    i = np.arange(P)
    r, c = i[:, None], i[None, :]
    consts = np.stack([r == c, np.ones((P, P)), r <= c, r >= c]).astype(np.float32)
    masks = np.zeros((2, 7, P, P), np.uint32)
    for lv in range(7):
        b = 1 << lv
        masks[0, lv] = (r // b % 2 == 1) & (c // b == r // b - 1)
        masks[1, lv] = masks[0, lv].T
    inv = np.zeros((NG, T), np.float32)

    def counts(n, w):
        t = np.arange(n)
        return np.clip(t + w // 2, 0, n) - np.clip(t - w // 2, 0, n)

    for g, w in enumerate(WINDOWS):
        inv[g, :CTX] = 1.0 / counts(CTX, w)
        inv[g, CTX:] = (1.0 / (counts(GRID_H, w)[:, None] * counts(GRID_W, w)[None, :])).ravel()
    return {"consts": consts, "masks": masks, "inv_count": inv}


def kernel(**inputs):
    import concourse.bacc as bacc
    from concourse.bass_utils import run_bass_kernel_spmd

    nc = bacc.Bacc("TRN2", target_bir_lowering=False, num_devices=1)
    arrays, a = {}, {}
    given = {n: np.ascontiguousarray(inputs[n]) for n in _INS} | shape_constants()
    for name, x in given.items():
        arrays[f"in_{name}"] = x
        a[name] = nc.dram_tensor(f"in_{name}", x.shape, mybir.dt.from_np(x.dtype), kind="ExternalInput").ap()
    outs = [nc.dram_tensor(f"out_{i}", s, F32, kind="ExternalOutput").ap() for i, s in enumerate(_OUTS)]
    build(nc, a, *outs)
    r = run_bass_kernel_spmd(nc, [arrays], core_ids=[0])
    return tuple(r.results[0][f"out_{i}"] for i in range(len(_OUTS)))
```

```python
from contextlib import ExitStack

import numpy as np
import concourse.bass as bass
from concourse import mybir

ALU = mybir.AluOpType
ACT = mybir.ActivationFunctionType
F32 = mybir.dt.float32
F16 = mybir.dt.float16
U32 = mybir.dt.uint32
AX_X = mybir.AxisListType.X

P = 128
D = 1024
KD = D // P
CTX, LAT = 128, 1024
T = CTX + LAT
NT = T // P
H = 8
NG = 4
WINDOWS = (2, 4, 8, 16)
GRID_W = 64
GRID_H = LAT // GRID_W
TAPS = 5
PAD = TAPS // 2
E = 16
CAP_L, CAP_C = 2 * LAT // E, 2 * CTX // E
CAP = CAP_L + CAP_C
EPS = 1e-6
OFF_POOL = 0
OFF_Q = NG * P
OFF_K = OFF_Q + D
OFF_V = OFF_K + D
OFF_G = OFF_V + D
OFF_BETA = OFF_G + D
OFF_ALPHA = OFF_BETA + 2 * H
OFF_MERGE = OFF_ALPHA + 2 * H
IN_COLS = OFF_MERGE + 2 * D
LEVELS = (2, 4, 8, 16, 32, 64)
PW = CTX + LAT + 4 * PAD
CW = PW - 2 * PAD
LAT0 = CTX + 2 * PAD

ROW_ADA_B, ROW_NORM1, ROW_PSCALE, ROW_ONORM, ROW_CCTX, ROW_C = 0, 48, 56, 60, 61, 69
N_ROWS = 77
CONV_ROWS = TAPS * 3 * H

ONCE = {
    "pe": ["cols_T", "mod1_T", "bd_filled", "bd_T", "gsum_filled", "gT_filled", "mod2_T", "affT_filled", "topkT_filled"],
    "act": ["silu_c_ready", "x_std", "sig_exp", "softplus_ln", "g_exp", "route_exp"],
    "dve": ["cols_ready", "x_rstd", "modT_ready", "bdT_ready", "absz", "g_ready", "gc_ready",
            "gT_ready", "gate2_ready", "halo_zero", "amp2_ready", "route_shift", "aff_ready", "topk_ready", "routes_ready"],
}


def tcol(t):
    return 0 if t == 0 else LAT0 + (t - 1) * P


def build(nc, a, out_p, out_s, out_sf, out_sb, dbg=None, stop=99):
    ctx = ExitStack()
    with ctx:
        sems = {}

        def sem(name):
            if name not in sems:
                sems[name] = ctx.enter_context(nc.semaphore(name))
            return sems[name]

        def reach(step):
            return sem(next(f"{e}_once" for e, steps in ONCE.items() if step in steps)), 1

        def at_step(step):
            e = next(e for e, steps in ONCE.items() if step in steps)
            return sem(f"{e}_once"), ONCE[e].index(step) + 1

        WORDS = (nc.sbuf_usable_end - nc.sbuf_base) // 4 - 64
        arena = ctx.enter_context(nc.sbuf_tensor("arena", [P, WORDS], F32))
        banks = [ctx.enter_context(nc.psum_tensor(f"bank{i}", [P, 512], F32)) for i in range(8)]
        at_word = [0]

        def take(n):
            o = at_word[0]
            at_word[0] += n
            assert at_word[0] <= WORDS, (at_word[0], WORDS)
            return arena[:, o:o + n]

        mod_dram = nc.dram_tensor("mod_dram", (2, 6 * D), F32).ap()
        b_dram = nc.dram_tensor("b_dram", (H * P, T), F32).ap()
        g_dram = nc.dram_tensor("g_dram", (2 * H, T), F32).ap()
        h2_dram = nc.dram_tensor("h2_dram", (T, D), F32).ap()
        x2_dram = nc.dram_tensor("x2_dram", (T, D), F32).ap()

        ident, ones, tri_f, tri_b = (take(P) for _ in range(4))
        ident_h, nident_h = (take(P // 2).bitcast(F16) for _ in range(2))
        mask_words = take(2 * 7 * P)
        masks = mask_words.bitcast(U32).rearrange("p (s l c) -> p s l c", s=2, l=7)
        cols = take(N_ROWS)
        conv_w = take(CONV_ROWS)
        silu_c = take(2 * KD)
        modT = take(2 * 48)
        amp1 = take(2 * KD)
        small = take(32)
        eps_c, qscale_c, one_c = small[:, 0:1], small[:, 1:2], small[:, 2:3]
        tab = {n: take(NT * 2 * H).rearrange("p (t d) -> p t d", t=NT)
               for n in ("beta", "nbeta", "g", "gc", "nbeg", "kd", "dl", "tmp", "tmp2")}
        PERSIST = at_word[0]
        hT = take(KD * T)
        hT3 = hT.rearrange("p (k t) -> p k t", k=KD)
        BT_AT = at_word[0]
        bT = take(KD * T)
        HEADS_AT = at_word[0]

        block = ctx.enter_context(nc.Block())
        progs = {"sync": [], "scalar": [], "vector": [], "gpsimd": [], "tensor": []}

        at_word[0] = BT_AT
        x_all = take(NT * D).rearrange("p (t d) -> p t d", t=NT)
        at_word[0] = HEADS_AT
        ada_slot = [take(KD * D).rearrange("p (k n) -> p k n", k=KD) for _ in range(2)]
        rows_in = take(P)
        convr_in = take(P)
        mod_r1, mod_r2 = take(P), take(P)
        mod_rows = take(6 * D)

        ada_rows = a["ada_b"].rearrange("l (r p) -> (l r) p", p=P)
        modT3 = modT.rearrange("p (c m) -> p c m", c=2)
        cols2 = cols[:, ROW_CCTX:ROW_CCTX + 16].rearrange("p (c k) -> p c k", c=2)
        silu3 = silu_c.rearrange("p (c k) -> p c k", c=2)
        amp3 = amp1.rearrange("p (c k) -> p c k", c=2)
        NG_ADA = 6
        ADA_BANKS = (1, 7)

        def load_ada(sp, g):
            sp.dma_start(ada_slot[g % 2], a["ada_w"][0].rearrange("(k p) n -> p k n", p=P)[:, :, g * D:(g + 1) * D]).then_inc(sem(f"ada_in{g % 2}"), 16)

        def sync1(sp):
            for i, name in enumerate(("ident", "ones", "tri_f", "tri_b")):
                sp.dma_start((ident, ones, tri_f, tri_b)[i], a["consts"][i]).then_inc(sem("consts_in"), 16)
            sp.dma_start(masks, a["masks"].rearrange("s l p c -> p s l c")).then_inc(sem("consts_in"), 16)
            for src, row in ((ada_rows, ROW_ADA_B), (a["norm1_g"].rearrange("l (r p) -> (l r) p", p=P), ROW_NORM1),
                             (a["pool_scale"].rearrange("l (r p) -> (l r) p", p=P), ROW_PSCALE),
                             (a["dn_onorm_g"], ROW_ONORM),
                             (a["c_ctx"].rearrange("(r p) -> r p", p=P), ROW_CCTX),
                             (a["c"].rearrange("b (r p) -> (b r) p", p=P), ROW_C)):
                sp.dma_start(rows_in[row:row + src.shape[0], :], src).then_inc(sem("consts_in"), 16)
            sp.dma_start(convr_in[0:CONV_ROWS, :], a["dn_conv"].rearrange("l t (j p) -> (l t j) p", p=P)).then_inc(sem("consts_in"), 16)
            sp.dma_start(mod_rows[0:2, :], a["ada_b"].to_broadcast([2, 6 * D])).then_inc(sem("adab_in"), 16)
            load_ada(sp, 0)
            sp.dma_start(x_all[:, 0, :], a["x_prompt"][0]).then_inc(sem("x_in"), 16)
            for t in range(1, NT):
                sp.dma_start(x_all[:, t, :], a["x_sample"][0, (t - 1) * P:t * P, :]).then_inc(sem("x_in"), 16)
            load_ada(sp, 1)
            for g in range(2, NG_ADA):
                sp.wait_ge(sem("ada_used"), g - 1)
                load_ada(sp, g)
                if g == 3:
                    sp.wait_ge(sem("mod_drained"), 2)
                    sp.dma_start(mod_dram[:, 0:2 * D], mod_rows[0:2, 0:2 * D]).then_inc(sem("mod_saved"), 16)
                    sp.wait_ge(sem("mod_saved"), 16)
                    for c in range(2):
                        sp.dma_start(mod_r1[c * 16:(c + 1) * 16, :], mod_dram[c, 0:2 * D].rearrange("(m p) -> m p", p=P)).then_inc(sem("mod_r1_in"), 16)

        N_CONSTS = 12 * 16

        def ada_group(pe, g):
            pe.wait_ge(sem(f"ada_in{g % 2}"), 16 * (g // 2 + 1))
            if g > 0:
                pe.wait_ge(sem("mod_drained"), g)
            for half_ in range(2):
                for k in range(KD):
                    last = nc.tensor.matmul(banks[ADA_BANKS[half_]][0:2, 0:512], silu3[:, :, k], ada_slot[g % 2][:, k, half_ * 512:(half_ + 1) * 512],
                                            start=(k == 0), stop=(k == KD - 1))
            last.then_inc(sem("ada_used"), 1)

        def mod_evac(dve, g):
            dve.wait_ge(sem("ada_used"), g + 1)
            for half_ in range(2):
                o = g * D + half_ * 512
                last = nc.vector.tensor_tensor(mod_rows[0:2, o:o + 512], banks[ADA_BANKS[half_]][0:2, 0:512], mod_rows[0:2, o:o + 512], ALU.add)
            last.then_inc(sem("mod_drained"), 1)

        H_USES = [(0, k, 0) for k in range(KD)] + [(1, k, half_) for half_ in range(2) for k in range(KD)]
        HB = 5

        def transpose_x(pe):
            for j, (c, k, half_) in enumerate(H_USES):
                if j >= HB:
                    pe.wait_ge(sem("hT_drained"), j - HB + 1)
                tiles = [0] if c == 0 else [1 + 4 * half_ + i for i in range(4)]
                pe.wait_ge(sem("xn_ready"), tiles[-1] + 1)
                for i, t in enumerate(tiles):
                    last = nc.tensor.transpose(banks[2 + j % HB][:, i * P:(i + 1) * P], x_all[:, t, k * P:(k + 1) * P], ident)
                last.then_inc(sem("xT_filled"), 1)

        def modulate_x(act):
            act.wait_ge(*at_step("modT_ready"))
            for j, (c, k, half_) in enumerate(H_USES):
                act.wait_ge(sem("xT_filled"), j + 1)
                n, at = (CTX, 0) if c == 0 else (512, CTX + 512 * half_)
                nc.scalar.activation(hT3[:, k, at:at + n], banks[2 + j % HB][:, 0:n], ACT.Identity,
                                     scale=amp3[:, c, k:k + 1], bias=modT3[:, c, k:k + 1]).then_inc(sem("hT_drained"), 1)

        w_bd = take(KD * 4 * H).rearrange("p (k n) -> p k n", k=KD)
        bias_rows = take(2 * H)
        alog_rows = take(2 * H)
        gT_rows = take(T)
        bdT = take(T)
        tokcols = banks[0][:, 0:NT * 32].rearrange("p (t n) -> p t n", t=NT)
        SPAN3 = ((0, CTX), (CTX, 512), (CTX + 512, 512))

        def sync3(sp):
            sp.dma_start(w_bd, a["w_in"][0].rearrange("(k p) n -> p k n", p=P)[:, :, OFF_BETA:OFF_MERGE]).then_inc(sem("bd_in"), 16)
            sp.dma_start(bias_rows, a["dn_dt_bias"].rearrange("l d h -> l (d h)").to_broadcast([P, 2 * H])).then_inc(sem("bd_in"), 16)
            sp.dma_start(alog_rows, a["dn_a_log"].rearrange("l d h -> l (d h)").to_broadcast([P, 2 * H])).then_inc(sem("bd_in"), 16)
            sp.wait_ge(*at_step("gT_ready"))
            sp.dma_start(g_dram, gT_rows[0:2 * H, :]).then_inc(sem("g_saved"), 16)
            sp.wait_ge(sem("mod_drained"), NG_ADA)
            sp.dma_start(mod_dram[:, 2 * D:6 * D], mod_rows[0:2, 2 * D:6 * D]).then_inc(sem("mod_saved"), 16)
            sp.wait_ge(sem("mod_saved"), 32)
            for c in range(2):
                sp.dma_start(mod_r2[c * KD:(c + 1) * KD, :], mod_dram[c, 5 * D:6 * D].rearrange("(m p) -> m p", p=P)).then_inc(sem("mod_r2_in"), 16)
            sp.wait_ge(sem("g_saved"), 16)

        def pe1(pe):
            pe.wait_ge(sem("consts_in"), N_CONSTS)
            nc.tensor.transpose(banks[0][:, 0:N_ROWS], rows_in[0:N_ROWS, :], ident[0:N_ROWS, 0:N_ROWS])
            nc.tensor.transpose(banks[0][:, 128:128 + CONV_ROWS], convr_in[0:CONV_ROWS, :], ident[0:CONV_ROWS, 0:CONV_ROWS]).then_inc(*reach("cols_T"))
            pe.wait_ge(*at_step("silu_c_ready"))
            for g in range(3):
                ada_group(pe, g)
            pe.wait_ge(sem("mod_r1_in"), 32)
            nc.tensor.transpose(banks[0][:, 256:288], mod_r1[0:32, :], ident[0:32, 0:32]).then_inc(*reach("mod1_T"))
            transpose_x(pe)
            ada_group(pe, 3)
            pe.wait_ge(sem("bd_in"), 48)
            pe.wait_ge(sem("hT_drained"), len(H_USES))
            for b, (at, n) in enumerate(SPAN3):
                for k in range(KD):
                    last = nc.tensor.matmul(banks[2 + b][0:4 * H, 0:n], w_bd[:, k, :], hT3[:, k, at:at + n], start=(k == 0), stop=(k == KD - 1))
            last.then_inc(*reach("bd_filled"))
            pe.wait_ge(*at_step("bdT_ready"))
            for t in range(NT):
                last = nc.tensor.transpose(tokcols[:, t, :], bdT[0:4 * H, t * P:(t + 1) * P], ident[0:4 * H, 0:4 * H])
            last.then_inc(*reach("bd_T"))
            ada_group(pe, 4)
            pe.wait_ge(*at_step("g_ready"))
            for d, tri in enumerate((tri_f, tri_b)):
                nc.tensor.matmul(banks[2][:, d * NT * H:(d + 1) * NT * H], tri, tab["g"][:, :, d * H:(d + 1) * H], start=True, stop=True)
            nc.tensor.matmul(banks[3][:, 0:NT * 2 * H], ones, tab["g"].rearrange("p t d -> p (t d)"), start=True, stop=True).then_inc(*reach("gsum_filled"))
            pe.wait_ge(*at_step("gc_ready"))
            for t in range(NT):
                last = nc.tensor.transpose(banks[4 + t // 3][0:2 * H, (t % 3) * P:(t % 3 + 1) * P], tab["gc"][:, t, :], ident)
            last.then_inc(*reach("gT_filled"))
            ada_group(pe, 5)

        def pe_gate2(pe):
            pe.wait_ge(sem("mod_r2_in"), 32)
            nc.tensor.transpose(banks[0][:, 0:2 * KD], mod_r2[0:2 * KD, :], ident[0:2 * KD, 0:2 * KD]).then_inc(*reach("mod2_T"))

        def act1(act):
            act.wait_ge(*at_step("cols_ready"))
            nc.scalar.activation(silu3, cols2, ACT.Silu).then_inc(*reach("silu_c_ready"))
            act.wait_ge(sem("x_in"), 16 * NT)
            act.wait_ge(sem("adab_in"), 16)
            for t in range(NT):
                last = nc.scalar.activation(bdT[:, 0:D], x_all[:, t, :], ACT.Square, accum_out=small[:, 8 + t:9 + t])
                last.then_inc(sem("act_order"), 1)
                act.wait_ge(sem("act_order"), t + 1)
            nc.scalar.activation(small[:, 20:20 + NT], small[:, 8:8 + NT], ACT.Sqrt, scale=1.0 / D, bias=eps_c).then_inc(*reach("x_std"))
            modulate_x(act)
            act.wait_ge(*at_step("bd_T"))
            nc.scalar.activation(tab["beta"], tokcols[:, :, 0:2 * H], ACT.Exp, scale=-1.0)
            act.wait_ge(sem("bd_in"), 48)
            nc.scalar.activation(alog_rows, alog_rows, ACT.Exp).then_inc(*reach("sig_exp"))
            act.wait_ge(*at_step("absz"))
            nc.scalar.activation(tab["tmp2"], tab["tmp2"], ACT.Exp, scale=-1.0).then_inc(sem("act_order"), 1)
            act.wait_ge(sem("act_order"), NT + 1)
            nc.scalar.activation(tab["tmp2"], tab["tmp2"], ACT.Ln, bias=one_c).then_inc(*reach("softplus_ln"))
            act.wait_ge(*at_step("gc_ready"))
            nc.scalar.activation(tab["kd"], tab["kd"], ACT.Exp)
            nc.scalar.activation(tab["dl"], tab["tmp"], ACT.Exp)
            nc.scalar.activation(tab["nbeg"], tab["gc"], ACT.Exp).then_inc(*reach("g_exp"))

        def dve1(dve):
            n = [0]

            def step(ins):
                n[0] += 1
                ins.then_inc(sem("dve_decay"), 1)
                dve.wait_ge(sem("dve_decay"), n[0])

            nc.vector.memset(eps_c, EPS)
            nc.vector.memset(qscale_c, -0.5 * float(np.log(P)))
            nc.vector.memset(one_c, 1.0)
            dve.wait_ge(*at_step("cols_T"))
            nc.vector.tensor_copy(cols, banks[0][:, 0:N_ROWS])
            nc.vector.tensor_copy(conv_w, banks[0][:, 128:128 + CONV_ROWS]).then_inc(*reach("cols_ready"))
            dve.wait_ge(sem("adab_in"), 16)
            mod_evac(dve, 0)
            dve.wait_ge(*at_step("x_std"))
            nc.vector.reciprocal(small[:, 8:8 + NT], small[:, 20:20 + NT]).then_inc(*reach("x_rstd"))
            dve.wait_ge(*at_step("x_rstd"))
            for t in range(NT):
                nc.vector.tensor_scalar(x_all[:, t, :], x_all[:, t, :], small[:, 8 + t:9 + t], None, ALU.mult).then_inc(sem("xn_ready"), 1)
            mod_evac(dve, 1)
            mod_evac(dve, 2)
            dve.wait_ge(*at_step("mod1_T"))
            for c in range(2):
                nc.vector.tensor_copy(modT3[:, c, 0:2 * KD], banks[0][:, 256 + c * 16:256 + (c + 1) * 16]).then_inc(sem("dve_mod"), 1)
            dve.wait_ge(sem("dve_mod"), 2)
            for c in range(2):
                last = nc.vector.scalar_tensor_tensor(amp3[:, c, :], modT3[:, c, KD:2 * KD], 1.0,
                                                      cols[:, ROW_NORM1:ROW_NORM1 + KD], ALU.add, ALU.mult)
            last.then_inc(*reach("modT_ready"))
            mod_evac(dve, 3)
            dve.wait_ge(*at_step("bd_filled"))
            for b, (at, n_) in enumerate(SPAN3):
                last = nc.vector.tensor_copy(bdT[0:4 * H, at:at + n_], banks[2 + b][0:4 * H, 0:n_])
            last.then_inc(*reach("bdT_ready"))
            dve.wait_ge(*at_step("sig_exp"))
            step(nc.vector.tensor_scalar(tab["beta"], tab["beta"], 1.0, None, ALU.add))
            step(nc.vector.reciprocal(tab["beta"], tab["beta"]))
            nc.vector.tensor_scalar(tab["nbeta"], tab["beta"], -1.0, None, ALU.mult)
            step(nc.vector.tensor_tensor(tab["tmp"], tokcols[:, :, 2 * H:4 * H], bias_rows.unsqueeze(1).to_broadcast([P, NT, 2 * H]), ALU.add))
            step(nc.vector.tensor_scalar(tab["tmp2"], tab["tmp"], -1.0, None, ALU.mult))
            nc.vector.tensor_tensor(tab["tmp2"], tab["tmp2"], tab["tmp"], ALU.max).then_inc(*reach("absz"))
            dve.wait_ge(*at_step("softplus_ln"))
            step(nc.vector.scalar_tensor_tensor(tab["g"], tab["tmp"], 0.0, tab["tmp2"], ALU.max, ALU.add))
            step(nc.vector.tensor_tensor(tab["g"], tab["g"], alog_rows.unsqueeze(1).to_broadcast([P, NT, 2 * H]), ALU.mult))
            nc.vector.tensor_scalar(tab["g"], tab["g"], -1.0, None, ALU.mult).then_inc(*reach("g_ready"))
            mod_evac(dve, 4)
            dve.wait_ge(*at_step("gsum_filled"))
            nc.vector.tensor_copy(tab["tmp"].rearrange("p t d -> p (t d)"), banks[3][:, 0:NT * 2 * H])
            for d in range(2):
                step(nc.vector.tensor_copy(tab["gc"][:, :, d * H:(d + 1) * H],
                                           banks[2][:, d * NT * H:(d + 1) * NT * H].rearrange("p (t h) -> p t h", h=H)))
            nc.vector.tensor_tensor(tab["kd"], tab["tmp"], tab["gc"], ALU.subtract).then_inc(*reach("gc_ready"))
            dve.wait_ge(*at_step("g_exp"))
            nc.vector.tensor_tensor(tab["nbeg"], tab["nbeg"], tab["nbeta"], ALU.mult)
            dve.wait_ge(*at_step("gT_filled"))
            for b in range(3):
                last = nc.vector.tensor_copy(gT_rows[0:2 * H, b * 384:(b + 1) * 384], banks[4 + b][0:2 * H, 0:384])
            last.then_inc(*reach("gT_ready"))
            mod_evac(dve, 5)

        def dve_gate2(dve):
            dve.wait_ge(*at_step("mod2_T"))
            for c in range(2):
                last = nc.vector.tensor_copy(modT3[:, c, 5 * KD:6 * KD], banks[0][:, c * KD:(c + 1) * KD])
            last.then_inc(*reach("gate2_ready"))

        at_word[0] = BT_AT
        w_head = [take(KD * P).rearrange("p (k n) -> p k n", k=KD) for _ in range(4)]
        raw = [take(PW) for _ in range(3)]
        qkvg = [take(PW) for _ in range(4)]
        qT, kT, vT, gateT = qkvg
        v3 = lambda x: x.rearrange("p (t c) -> p t c", t=NT)
        half = lambda: v3(take(T // 2).bitcast(F16))
        grow = [take(T) for _ in range(2)]
        dm_flat = [take(T) for _ in range(2)]
        kq_flat = [take(T) for _ in range(2)]
        dm, kq = [v3(x) for x in dm_flat], [v3(x) for x in kq_flat]
        attnT = [v3(take(T)) for _ in range(2)]
        ktok, vtok = v3(take(T)), v3(take(T))
        vb = [v3(take(T)) for _ in range(2)]
        Yf = [v3(take(T)) for _ in range(2)]
        nL, nLlo = [half() for _ in range(2)], [half() for _ in range(2)]
        Xs, Ys, Zs = ([half() for _ in range(2)] for _ in range(3))
        S = [[take(P) for _ in range(2)] for _ in range(2)]
        scan = dm_flat[0][:, 0:6 * P].rearrange("p (s d c) -> p s d c", s=3, d=2)
        orow = small[:, 8:8 + NT]
        TRI = (banks[0:3], banks[3:6])
        USES = {0: ["nq", "kT", "kk"], 1: ["nk", "vT", "kq"]}
        for d in range(2):
            USES[d] += ["LT", "Y2"]
            for b in LEVELS:
                USES[d] += [f"Z{b}", f"P{b}", f"X{b}"]
            USES[d] += ["res", "fix"]
        USES[0] += ["oT"]
        BY_DVE = {(d, n) for d in range(2) for n in ["vT", "LT", "oT", "fix"] + [f"P{b}" for b in LEVELS]}
        BY_DVE |= {(1, "res")} | {(1, f"Z{b}") for b in LEVELS}

        def use(d, name):
            return USES[d].index(name)

        def filled(eng, h, d, name, g):
            eng.wait_ge(sem(f"filled{d}"), h * (3 * len(USES[d])) + 3 * use(d, name) + g + 1)

        def drained_sem(d, name):
            return sem(f"drained{d}_{'dve' if (d, name) in BY_DVE else 'act'}")

        def drained_count(h, d, name, g):
            mine = [n for n in USES[d] if ((d, n) in BY_DVE) == ((d, name) in BY_DVE)]
            return h * (3 * len(mine)) + 3 * mine.index(name) + g + 1

        def drained(eng, h, d, name, g):
            before = USES[d][use(d, name) - 1]
            eng.wait_ge(drained_sem(d, before), drained_count(h, d, before, g))

        def all_drained(eng, h, d, name):
            eng.wait_ge(drained_sem(d, name), drained_count(h, d, name, 2))

        def alone(eng):
            eng.sem_inc(sem("waits_kept"), 1)

        def tile_at(d, t):
            return t if d == 0 or t == 0 else NT - t

        SPAN = ((0, CTX), (CTX, 512), (CTX + 512, 512))
        UNITS = 12
        LEVELS_AT = 52
        MATS = (3, 0, 2, 1)
        LT_AT = 5 * KD + 4

        def unit_count(h, u):
            return UNITS * (h + 1) + u - 2

        def project(pe, h, i0, i1):
            for i in range(i0, i1):
                u, k = i // KD, i % KD
                at, n = SPAN[u % 3]
                m = MATS[u // 3]
                if k == 0:
                    if u % 3 == 0:
                        pe.wait_ge(sem(f"w_in{m}"), 16 * (h + 1 if m == 3 else h + 2))
                    if not (isinstance(h, int) and h == -1 and u < 5):
                        pe.wait_ge(sem("pj_drained"), unit_count(h, u) - 2)
                ins = nc.tensor.matmul(banks[6 + u % 2][:, 0:n], w_head[m][:, k, :], hT3[:, k, at:at + n], start=(k == 0), stop=(k == KD - 1))
                if k == KD - 1:
                    ins.then_inc(sem("pj_filled"), 1)

        SPANS_RAW = (PAD, LAT0 + PAD, LAT0 + PAD + 512)
        SPANS_CONV = (0, LAT0, LAT0 + 512)

        def evac_unit(act, h, u):
            n = SPAN[u % 3][1]
            act.wait_ge(sem("pj_filled"), unit_count(h, u))
            if u < 3:
                dst = gateT[:, SPANS_CONV[u]:SPANS_CONV[u] + n]
            else:
                at = SPANS_RAW[u % 3]
                dst = raw[MATS[u // 3]][:, at:at + n]
            nc.scalar.activation(dst, banks[6 + u % 2][:, 0:n], ACT.Copy).then_inc(sem("pj_drained"), 1)

        def load_w(sp, h, j):
            off = (OFF_Q, OFF_K, OFF_V, OFF_G)[j]
            sp.dma_start(w_head[j], a["w_in"][0].rearrange("(k p) n -> p k n", p=P)[:, :, bass.ds(off + h * P, P)]).then_inc(sem(f"w_in{j}"), 16)

        def load_decay_and_state(sp, h):
            for d in range(2):
                sp.dma_start(grow[d], g_dram[bass.ds(h + d * H, 1), :].to_broadcast([P, T])).then_inc(sem(f"grow_in{d}"), 16)
                sp.dma_start(S[d][1], (a["state_dn_fwd"], a["state_dn_bwd"])[d].rearrange("b l h k v -> (b l h k) v")[bass.ds(h * P, P), :]).then_inc(sem(f"S_in{d}"), 16)

        def store_states(sp, h):
            for d in range(2):
                sp.wait_ge(sem(f"S_upd{d}"), h * (NT + 1) + 2)
                sp.dma_start((out_sf, out_sb)[d].rearrange("b l h k v -> (b l h k) v")[bass.ds(h * P, P), :], S[d][0]).then_inc(sem(f"S_out{d}"), 16)

        def store_b(sp, h):
            sp.wait_ge(sem("b_ready"), h + 1)
            sp.dma_start(b_dram[bass.ds(h * P, P), :], kq_flat[1]).then_inc(sem("b_out"), 16)

        def sync4(sp):
            sp.wait_ge(sem("scan_done"), 1)
            sp.dma_start(small[0:1, 29:32], a["consts"][0][0:1, 0:3]).then_inc(sem("b_out"), 16)
            for j in range(4):
                load_w(sp, 0, j)
            load_decay_and_state(sp, 0)
            with sp.Fori(0, H - 1) as h:
                sp.wait_ge(sem("pj_filled"), unit_count(h - 1, UNITS - 1))
                for j in range(3):
                    load_w(sp, h + 1, j)
                sp.wait_ge(sem("pj_filled"), unit_count(h, 2))
                load_w(sp, h + 1, 3)
                store_states(sp, h)
                store_b(sp, h)
                sp.wait_ge(sem("scan_done"), h + 2)
                load_decay_and_state(sp, h + 1)
            store_states(sp, H - 1)
            store_b(sp, H - 1)

        def body_pe(pe, h, last_h=False):
            fill = (lambda *x: None) if last_h else (lambda i0, i1: project(pe, h, i0, i1))
            project(pe, h, 2 * KD, 3 * KD)
            pe.wait_ge(sem("scan_done"), h + 1)
            for d, name in enumerate(("nq", "nk")):
                pe.wait_ge(sem("sq_ready"), 2 * h + d + 1)
                for b, (at, n) in enumerate(SPAN):
                    nc.tensor.matmul(TRI[d][b][:, 0:n], ones, dm_flat[d][:, at:at + n], start=True, stop=True).then_inc(sem(f"filled{d}"), 1)
                fill(*((24, 32), (32, 40))[d])
            for d, name in ((1, "vT"), (0, "kT")):
                pe.wait_ge(sem("k_normed" if d == 0 else "v_ready"), h + 1)
                for g in range(3):
                    drained(pe, h, d, name, g)
                    for i in range(3):
                        last = nc.tensor.transpose(TRI[d][g][:, i * P:(i + 1) * P], (kT, vT)[d][:, tcol(3 * g + i):tcol(3 * g + i) + P], ident)
                    last.then_inc(sem(f"filled{d}"), 1)
            for d, name in enumerate(("kk", "kq")):
                if d == 1:
                    pe.wait_ge(sem("q_normed"), h + 1)
                for g in range(3):
                    drained(pe, h, d, name, g)
                    for i in range(3):
                        at = tcol(3 * g + i)
                        last = nc.tensor.matmul(TRI[d][g][:, i * P:(i + 1) * P], kT[:, at:at + P], (kT, qT)[d][:, at:at + P], start=True, stop=True)
                    last.then_inc(sem(f"filled{d}"), 1)
            fill(5 * KD, LT_AT)
            for d in range(2):
                for g in range(3):
                    pe.wait_ge(sem("lt_ready"), 6 * h + 3 * d + g + 1)
                    drained(pe, h, d, "LT", g)
                    for i in range(3):
                        last = nc.tensor.transpose(TRI[d][g][:, i * P:(i + 1) * P], Yf[d][:, 3 * g + i, :], ident)
                    last.then_inc(sem(f"filled{d}"), 1)

            def turn(d, name, src):
                for g in range(3):
                    drained(pe, h, d, name, g)
                    for i in range(3):
                        last = nc.tensor.transpose(TRI[d][g].bitcast(F16)[:, i * P:(i + 1) * P], src[d][:, 3 * g + i, :], ident_h)
                    last.then_inc(sem(f"filled{d}"), 1)

            def products(d, name, terms):
                for g in range(3):
                    drained(pe, h, d, name, g)
                    for i in range(3):
                        for n, (lhs, rhs) in enumerate(terms):
                            last = nc.tensor.matmul(TRI[d][g][:, i * P:(i + 1) * P], lhs if lhs.shape[1] == P else lhs[:, 3 * g + i, :],
                                                    rhs if rhs.shape[1] == P else rhs[:, 3 * g + i, :],
                                                    start=(n == 0), stop=(n == len(terms) - 1))
                    last.then_inc(sem(f"filled{d}"), 1)

            fill(LT_AT, LEVELS_AT)
            for d in range(2):
                pe.wait_ge(sem("X_init"), 6 * h + 3 * d + 3)
                turn(d, "Y2", Xs)
            for lv, b in enumerate(LEVELS):
                for d in range(2):
                    products(d, f"Z{b}", [(nL[d], Ys[d])])
                fill(LEVELS_AT + 4 * lv, LEVELS_AT + 4 * lv + 2)
                for d in range(2):
                    products(d, f"P{b}", [(Xs[d], Zs[d])])
                fill(LEVELS_AT + 4 * lv + 2, LEVELS_AT + 4 * lv + 4)
                for d in range(2):
                    turn(d, f"X{b}", Ys)
            for d in range(2):
                pe.wait_ge(sem("nLlo_ready"), 2 * h + d + 1)
                products(d, "res", [(nL[d], Ys[d]), (nLlo[d], Ys[d]), (nident_h, Ys[d]), (ident_h, ident_h)])
            for d in range(2):
                products(d, "fix", [(Xs[d], Zs[d])])
            for d in range(2):
                all_drained(pe, h, d, "fix")
                pe.wait_ge(sem("qd_ready"), 2 * h + d + 1)
                pe.wait_ge(sem("attn_ready"), 2 * h + d + 1)
            slot = LEVELS_AT + 4 * len(LEVELS)
            scan_fills = [(t, i) for t in range(NT) for i in range(3)]
            n_fills = UNITS * KD - slot
            scan_fills = set(scan_fills[j * len(scan_fills) // n_fills] for j in range(n_fills))
            for t in range(NT):
                for d in range(2):
                    s, ti = S[d][min(t, 1)], tile_at(d, t)
                    at = tcol(ti)
                    pe.wait_ge(sem(f"S_upd{d}"), h * (NT + 1) + t + 1)
                    if t == 1:
                        pe.wait_ge(sem(f"S_in{d}"), 16 * h + 16)
                    nc.tensor.matmul(TRI[d][0][:, 0:P], kT[:, at:at + P], s, start=True, stop=True).then_inc(sem(f"kS_filled{d}"), 1)
                if (t, 0) in scan_fills:
                    fill(slot, slot + 1)
                    slot += 1
                for d in range(2):
                    pe.wait_ge(sem(f"R_ready{d}"), h * NT + t + 1)
                    nc.tensor.matmul(TRI[d][1][:, 0:P], Yf[d][:, tile_at(d, t), :], scan[:, 0, d, :], start=True, stop=True).then_inc(sem(f"vn_filled{d}"), 1)
                if (t, 1) in scan_fills:
                    fill(slot, slot + 1)
                    slot += 1
                for d in range(2):
                    s, ti = S[d][min(t, 1)], tile_at(d, t)
                    pe.wait_ge(sem(f"vn_ready{d}"), h * NT + t + 1)
                    nc.tensor.matmul(TRI[d][0][:, 0:P], ktok[:, ti, :], scan[:, 2, d, :], start=True, stop=True)
                    if t > 0:
                        pe.wait_ge(sem(f"o_drained{d}"), h * NT + t)
                    nc.tensor.matmul(TRI[d][2][:, 0:P], grow[d][:, ti * P:(ti + 1) * P], s, start=True, stop=False)
                    nc.tensor.matmul(TRI[d][2][:, 0:P], attnT[d][:, ti, :], scan[:, 1, d, :], start=False, stop=True).then_inc(sem(f"o_filled{d}"), 1)
                if (t, 2) in scan_fills:
                    fill(slot, slot + 1)
                    slot += 1
            if not last_h:
                project(pe, h + 1, 0, 2 * KD)
            pe.wait_ge(sem("o_normed"), h + 1)
            for g in range(3):
                for i in range(3):
                    last = nc.tensor.transpose(TRI[0][g][:, i * P:(i + 1) * P], kq[0][:, 3 * g + i, :], ident)
                last.then_inc(sem("filled0"), 1)

        def flat(x, g):
            return x[:, 3 * g:3 * g + 3, :].rearrange("p t c -> p (t c)")

        def body_act(act, h, last_h=False):
            evac = (lambda u: None) if last_h else (lambda u: evac_unit(act, h, u))

            def silu(j):
                if j < 3:
                    act.wait_ge(sem("conv_done"), 3 * h + MATS.index(j))
                else:
                    act.wait_ge(sem("pj_drained"), unit_count(h, 2))
                for n, at in ((CTX, 0), (LAT, LAT0)):
                    last = nc.scalar.activation(qkvg[j][:, at:at + n], qkvg[j][:, at:at + n], ACT.Silu)
                if j == 2:
                    last.then_inc(sem("v_ready"), 1)
                elif j == 3:
                    last.then_inc(sem("gate_ready"), 1)
                else:
                    last.then_inc(sem("qk_silu"), 1)
                    act.wait_ge(sem("qk_silu"), 2 * h + j + 1)
                    nc.scalar.activation(dm_flat[j][:, 0:CTX], qkvg[j][:, 0:CTX], ACT.Square)
                    nc.scalar.activation(dm_flat[j][:, CTX:T], qkvg[j][:, LAT0:LAT0 + LAT], ACT.Square).then_inc(sem("sq_ready"), 1)

            silu(0)
            silu(2)
            act.wait_ge(sem("scan_done"), h + 1)
            evac_unit(act, h, 0)
            evac_unit(act, h, 1)
            silu(1)
            evac_unit(act, h, 2)
            silu(3)
            evac(3)
            for d in range(2):
                for b, (at, n) in enumerate(SPAN):
                    filled(act, h, d, ("nq", "nk")[d], b)
                    nc.scalar.activation(dm_flat[d][:, at:at + n], TRI[d][b][:, 0:n], ACT.Ln, bias=eps_c).then_inc(sem(f"drained{d}_act"), 1)
            for d in (1, 0):
                all_drained(act, h, d, ("nq", "nk")[d])
                nc.scalar.activation(dm_flat[d], dm_flat[d], ACT.Exp, scale=-0.5, bias=qscale_c if d == 0 else 0.0).then_inc(sem("rnorm"), 1)
            evac(4)
            for g in range(3):
                filled(act, h, 0, "kT", g)
                nc.scalar.activation(flat(ktok, g), TRI[0][g][:, 0:384], ACT.Copy).then_inc(sem("drained0_act"), 1)
            act.wait_ge(sem("b_out"), 16 * h + 16)
            for d in range(2):
                for g in range(3):
                    filled(act, h, d, ("kk", "kq")[d], g)
                    nc.scalar.activation(kq_flat[d][:, g * 384:(g + 1) * 384], TRI[d][g][:, 0:384], ACT.Copy).then_inc(sem(f"drained{d}_act"), 1)
            for d in range(2):
                act.wait_ge(sem("gdiff"), 2 * h + d + 1)
                nc.scalar.activation(dm_flat[d], dm_flat[d], ACT.Exp).then_inc(sem("decay_exp"), 1)
            for d in range(2):
                nc.scalar.activation(grow[d], grow[d], ACT.Exp).then_inc(sem("grow_exp"), 1)
            for d in range(2):
                for g in range(3):
                    act.wait_ge(sem("nl_masked"), 6 * h + 3 * d + g + 1)
                    nc.scalar.activation(flat(nL[d], g), flat(Yf[d], g), ACT.Copy).then_inc(sem("nL_ready"), 1)
            evac(5)

            def copy(d, name, dst, dt=F32):
                for g in range(3):
                    filled(act, h, d, name, g)
                    src = TRI[d][g] if dt == F32 else TRI[d][g].bitcast(dt)
                    nc.scalar.activation(flat(dst[d], g), src[:, 0:384], ACT.Copy).then_inc(sem(f"drained{d}_act"), 1)

            for d in range(2):
                copy(d, "Y2", Ys, F16)
            for lv, b in enumerate(LEVELS):
                copy(0, f"Z{b}", Zs)
                for d in range(2):
                    copy(d, f"X{b}", Xs, F16)
                if lv % 2 == 1:
                    evac(6 + lv // 2)
            copy(0, "res", Zs)
            EVAC_AT = {2: 9, 5: 10, NT - 1: 11}
            for t in range(NT):
                for d in range(2):
                    ti = tile_at(d, t)
                    act.wait_ge(sem(f"vn_filled{d}"), h * NT + t + 1)
                    nc.scalar.activation(scan[:, 2, d, :], TRI[d][1][:, 0:P], ACT.Copy, scale=tab["kd"][:, ti, bass.ds(h + d * H, 1)])
                    nc.scalar.activation(scan[:, 1, d, :], TRI[d][1][:, 0:P], ACT.Copy).then_inc(sem(f"vn_ready{d}"), 1)
                for d in range(2):
                    act.wait_ge(sem(f"o_filled{d}"), h * NT + t + 1)
                    nc.scalar.activation(kq[d][:, tile_at(d, t), :], TRI[d][2][:, 0:P], ACT.Copy).then_inc(sem(f"o_drained{d}"), 1)
                if t in EVAC_AT:
                    evac(EVAC_AT[t])
            act.wait_ge(sem("o_sumsq"), h + 1)
            nc.scalar.activation(orow, orow, ACT.Ln, scale=1.0 / P, bias=eps_c).then_inc(sem("o_ln"), 1)
            act.wait_ge(sem("o_ln"), h + 1)
            nc.scalar.activation(orow, orow, ACT.Exp, scale=-0.5).then_inc(sem("o_rstd"), 1)

        def conv_tap(dve, h, j, tap):
            if tap == 0:
                dve.wait_ge(sem("pj_drained"), unit_count(h - 1, 3 * MATS.index(j) + 2))
            else:
                dve.wait_ge(sem("tap_done"), h * (3 * (TAPS - 1)) + (MATS.index(j) - 1) * (TAPS - 1) + tap)
            w = conv_w[:, bass.ds(tap * 3 * H + j * H + h, 1)]
            if tap == 0:
                ins = nc.vector.tensor_scalar(qkvg[j][:, 0:CW], raw[j][:, 0:CW], w, None, ALU.mult)
            else:
                ins = nc.vector.scalar_tensor_tensor(qkvg[j][:, 0:CW], raw[j][:, tap:tap + CW], w, qkvg[j][:, 0:CW], ALU.mult, ALU.add)
            ins.then_inc(sem("tap_done" if tap < TAPS - 1 else "conv_done"), 1)

        def body_dve(dve, h, last_h=False):
            for tap in range(TAPS):
                conv_tap(dve, h, 1, tap)
            for d, name in ((1, "k_normed"), (0, "q_normed")):
                dve.wait_ge(sem("rnorm"), 2 * h + 2 - d)
                nc.vector.tensor_tensor(qkvg[d][:, 0:CTX], qkvg[d][:, 0:CTX], dm_flat[d][:, 0:CTX], ALU.mult)
                nc.vector.tensor_tensor(qkvg[d][:, LAT0:LAT0 + LAT], qkvg[d][:, LAT0:LAT0 + LAT], dm_flat[d][:, CTX:T], ALU.mult).then_inc(sem(name), 1)
            for g in range(3):
                filled(dve, h, 1, "vT", g)
                nc.vector.tensor_copy(flat(vtok, g), TRI[1][g][:, 0:384]).then_inc(sem("drained1_dve"), 1)
            for d in range(2):
                dve.wait_ge(sem(f"grow_in{d}"), 16 * h + 16)
                dve.wait_ge(sem("q_normed" if d == 0 else "k_normed"), h + 1)
                for t in range(NT):
                    last = nc.vector.tensor_scalar(dm_flat[d][:, t * P:(t + 1) * P], grow[d][:, t * P:(t + 1) * P],
                                                   tab["gc"][:, t, bass.ds(h + d * H, 1)], 0.0, ALU.subtract, ALU.min)
                last.then_inc(sem("gdiff"), 1)
            for d in range(2):
                dve.wait_ge(sem("decay_masked"), 2 * h + d + 1)
                all_drained(dve, h, 0, "kk")
                for g in range(3):
                    nc.vector.tensor_tensor(Yf[d][:, 3 * g:3 * g + 3, :], kq[0][:, 3 * g:3 * g + 3, :], dm[d][:, 3 * g:3 * g + 3, :], ALU.mult).then_inc(sem("lt_ready"), 1)
            for d in range(2):
                nc.vector.tensor_copy(Xs[d], ident_h.unsqueeze(1).to_broadcast([P, NT, P])).then_inc(sem("X_eye"), 1)
            for d in range(2):
                for g in range(3):
                    filled(dve, h, d, "LT", g)
                    nc.vector.tensor_tensor(Yf[d][:, 3 * g:3 * g + 3, :], TRI[d][g][:, 0:384].rearrange("p (t c) -> p t c", t=3),
                                            tab["nbeta"][:, 3 * g:3 * g + 3, bass.ds(h + d * H, 1)].to_broadcast([P, 3, P]), ALU.mult).then_inc(sem(f"drained{d}_dve"), 1)
            for d in range(2):
                dve.wait_ge(sem("grow_exp"), 2 * h + d + 1)
                nc.vector.tensor_tensor(grow[d][:, 0:CTX], qT[:, 0:CTX], grow[d][:, 0:CTX], ALU.mult)
                nc.vector.tensor_tensor(grow[d][:, CTX:T], qT[:, LAT0:LAT0 + LAT], grow[d][:, CTX:T], ALU.mult).then_inc(sem("qd_ready"), 1)
            dve.wait_ge(sem("X_eye"), 2 * h + 2)
            for d in range(2):
                for g in range(3):
                    dve.wait_ge(sem("nL_ready"), 6 * h + 3 * d + g + 1)
                    alone(dve)
                    nc.vector.copy_predicated(Xs[d][:, 3 * g:3 * g + 3, :], masks[:, d, 0, :].unsqueeze(1).to_broadcast([P, 3, P]), nL[d][:, 3 * g:3 * g + 3, :]).then_inc(sem("X_init"), 1)

            def copy1(name):
                for g in range(3):
                    filled(dve, h, 1, name, g)
                    nc.vector.tensor_copy(flat(Zs[1], g), TRI[1][g][:, 0:384]).then_inc(sem("drained1_dve"), 1)

            for lv, b in enumerate(LEVELS):
                copy1(f"Z{b}")
                for d in range(2):
                    for g in range(3):
                        filled(dve, h, d, f"P{b}", g)
                        alone(dve)
                        nc.vector.copy_predicated(Ys[d][:, 3 * g:3 * g + 3, :], masks[:, 1 - d, lv + 1, :].unsqueeze(1).to_broadcast([P, 3, P]),
                                                  TRI[d][g][:, 0:384].rearrange("p (t c) -> p t c", t=3)).then_inc(sem(f"drained{d}_dve"), 1)
            copy1("res")
            for d in range(2):
                for g in range(3):
                    filled(dve, h, d, "fix", g)
                    nc.vector.tensor_tensor(flat(Yf[d], g), TRI[d][g][:, 0:384], flat(Ys[d], g), ALU.add).then_inc(sem(f"drained{d}_dve"), 1)
            for d in range(2):
                dve.wait_ge(sem("vb_ready"), 2 * h + d + 1)
            for t in range(NT):
                for d in range(2):
                    ti = tile_at(d, t)
                    dve.wait_ge(sem(f"kS_filled{d}"), h * NT + t + 1)
                    nc.vector.scalar_tensor_tensor(scan[:, 0, d, :], TRI[d][0][:, 0:P], tab["nbeg"][:, ti, bass.ds(h + d * H, 1)],
                                                   vb[d][:, ti, :], ALU.mult, ALU.add).then_inc(sem(f"R_ready{d}"), 1)
                if not last_h:
                    conv_tap(dve, h + 1, 2 * (t // TAPS), t % TAPS)
                for d in range(2):
                    ti = tile_at(d, t)
                    s = S[d][min(t, 1)]
                    dve.wait_ge(sem(f"o_filled{d}"), h * NT + t + 1)
                    nc.vector.scalar_tensor_tensor(s, s, tab["dl"][:, ti, bass.ds(h + d * H, 1)], TRI[d][0][:, 0:P], ALU.mult, ALU.add).then_inc(sem(f"S_upd{d}"), 1)
            if not last_h:
                conv_tap(dve, h + 1, 2, TAPS - 1)
            dve.wait_ge(sem("o_squared"), h + 1)
            nc.vector.tensor_reduce(orow, kq[1], AX_X, ALU.add).then_inc(sem("o_sumsq"), 1)
            dve.wait_ge(sem("o_rstd"), h + 1)
            nc.vector.tensor_tensor(kq[0], kq[0], orow.unsqueeze(2).to_broadcast([P, NT, P]), ALU.mult).then_inc(sem("o_normed"), 1)
            on = cols[:, ROW_ONORM:ROW_ONORM + 1]
            dve.wait_ge(sem("gate_ready"), h + 1)
            for g in range(3):
                filled(dve, h, 0, "oT", g)
                if g == 0:
                    nc.vector.scalar_tensor_tensor(kq_flat[1][:, 0:P], TRI[0][0][:, 0:P], on, gateT[:, 0:P], ALU.mult, ALU.mult)
                    nc.vector.scalar_tensor_tensor(kq_flat[1][:, P:3 * P], TRI[0][0][:, P:3 * P], on, gateT[:, LAT0:LAT0 + 2 * P], ALU.mult, ALU.mult).then_inc(sem("drained0_dve"), 1)
                else:
                    at = tcol(3 * g)
                    nc.vector.scalar_tensor_tensor(kq_flat[1][:, 3 * g * P:(3 * g + 3) * P], TRI[0][g][:, 0:3 * P], on, gateT[:, at:at + 3 * P], ALU.mult, ALU.mult).then_inc(sem("drained0_dve"), 1)
            nc.vector.memset(small[:, 5:6], 0.0).then_inc(sem("b_ready"), 1)
            nc.vector.memset(small[:, 3:4], 0.0).then_inc(sem("scan_done"), 1)
            for d in range(2):
                dve.wait_ge(sem(f"S_out{d}"), 16 * h + 16)
                nc.vector.memset(S[d][0], 0.0).then_inc(sem(f"S_upd{d}"), 1)

        def dve4_first(dve):
            dve.wait_ge(sem("hT_drained"), len(H_USES))
            dve.wait_ge(sem("g_saved"), 16)
            nc.vector.tensor_copy(ident_h, ident)
            nc.vector.tensor_scalar(nident_h, ident, -1.0, None, ALU.mult)
            for r in raw:
                nc.vector.memset(r[:, 0:PAD], 0.0)
                nc.vector.memset(r[:, PAD + CTX:LAT0 + PAD], 0.0)
                nc.vector.memset(r[:, PW - PAD:PW], 0.0)
            nc.vector.memset(small[:, 3:4], 0.0).then_inc(sem("scan_done"), 1)
            dve.wait_ge(sem("scan_done"), 1)
            for d in range(2):
                nc.vector.memset(S[d][0], 0.0).then_inc(sem(f"S_upd{d}"), 1)

        def body_pool(pool, h):
            for d in range(2):
                sgn = 1 - 2 * d
                pool.wait_ge(sem("decay_exp"), 2 * h + d + 1)
                alone(pool)
                nc.gpsimd.affine_select(out=dm[d], in_=dm[d], compare_op=ALU.is_ge, fill=0.0, base=0,
                                        pattern=[[0, NT], [sgn, P]], channel_multiplier=-sgn).then_inc(sem("decay_masked"), 1)
            for d in range(2):
                for g in range(3):
                    pool.wait_ge(drained_sem(d, "LT"), drained_count(h, d, "LT", g))
                    alone(pool)
                    nc.gpsimd.affine_select(out=Yf[d][:, 3 * g:3 * g + 3, :], in_=Yf[d][:, 3 * g:3 * g + 3, :], compare_op=ALU.not_equal, fill=0.0, base=0,
                                            pattern=[[0, 3], [-1, P]], channel_multiplier=1).then_inc(sem("nl_masked"), 1)
            for d in range(2):
                pool.wait_ge(sem("decay_masked"), 2 * h + d + 1)
                all_drained(pool, h, 1, "kq")
                nc.gpsimd.tensor_tensor(attnT[d], kq[1], dm[d], ALU.mult).then_inc(sem("attn_ready"), 1)
            for d in range(2):
                pool.wait_ge(sem("nL_ready"), 6 * h + 3 * d + 3)
                nc.gpsimd.tensor_tensor(nLlo[d], Yf[d], nL[d], ALU.subtract).then_inc(sem("nLlo_ready"), 1)
            for d in range(2):
                all_drained(pool, h, 1, "vT")
                nc.gpsimd.tensor_tensor(vb[d], vtok, tab["beta"][:, :, bass.ds(h + d * H, 1)].to_broadcast([P, NT, P]), ALU.mult).then_inc(sem("vb_ready"), 1)
            for d in range(2):
                pool.wait_ge(sem(f"o_drained{d}"), (h + 1) * NT)
            nc.gpsimd.tensor_tensor(kq[0], kq[0], kq[1], ALU.add).then_inc(sem("o_added"), 1)
            pool.wait_ge(sem("o_added"), h + 1)
            nc.gpsimd.tensor_tensor(kq[1], kq[0], kq[0], ALU.mult).then_inc(sem("o_squared"), 1)

        def prologue_pe(pe):
            pe.wait_ge(sem("scan_done"), 1)
            project(pe, -1, 3 * KD, 12 * KD)
            project(pe, 0, 0, 2 * KD)

        def prologue_act(act):
            act.wait_ge(sem("scan_done"), 1)
            for u in range(3, UNITS):
                evac_unit(act, -1, u)

        RES = dict(locals())
        from_later = later(nc, a, RES, out_p, out_s, dbg, stop)

        @block.sync
        def _(sp):
            sync1(sp)
            sync3(sp)
            if stop >= 4:
                sync4(sp)
            from_later["sync"](sp)

        @block.tensor
        def _(pe):
            pe1(pe)
            pe_gate2(pe)
            if stop >= 4:
                prologue_pe(pe)
                with pe.Fori(0, H - 1) as h:
                    body_pe(pe, h)
                body_pe(pe, H - 1, True)
            from_later["tensor"](pe)

        @block.scalar
        def _(act):
            act1(act)
            if stop >= 4:
                prologue_act(act)
                with act.Fori(0, H - 1) as h:
                    body_act(act, h)
                body_act(act, H - 1, True)
            from_later["scalar"](act)

        @block.vector
        def _(dve):
            dve1(dve)
            dve_gate2(dve)
            dve4_first(dve)
            if stop >= 4:
                for j in (0, 2):
                    for tap in range(TAPS):
                        conv_tap(dve, 0, j, tap)
                with dve.Fori(0, H - 1) as h:
                    body_dve(dve, h)
                body_dve(dve, H - 1, True)
            from_later["vector"](dve)

        @block.gpsimd
        def _(pool):
            if stop >= 4:
                with pool.Fori(0, H) as h:
                    body_pool(pool, h)
            from_later["gpsimd"](pool)


def later(nc, a, v, out_p, out_s, dbg, stop):
    alone, reach, at_step = v["alone"], v["reach"], v["at_step"]
    sem, take, at_word, banks, arena = v["sem"], v["take"], v["at_word"], v["banks"], v["arena"]
    ident, cols, modT3, small, eps_c = v["ident"], v["cols"], v["modT3"], v["small"], v["eps_c"]
    hT3, bT = v["hT3"], v["bT"]
    bT3 = bT.rearrange("p (k t) -> p k t", k=KD)
    HEADS_AT, BT_AT, PERSIST = v["HEADS_AT"], v["BT_AT"], v["PERSIST"]
    mod_dram, h2_dram, x2_dram = v["mod_dram"], v["h2_dram"], v["x2_dram"]
    w_in3 = a["w_in"][0].rearrange("(k p) n -> p k n", p=P)
    COLS = ((0, CTX), (CTX, 512), (CTX + 512, 512))

    at_word[0] = HEADS_AT
    p4 = take(NG * T).rearrange("p (g t) -> p g t", g=NG)
    MIX_AT = at_word[0]
    w_pool = take(KD * NG * P).rearrange("p (k n) -> p k n", k=KD)
    pool_w = take(NG * P).rearrange("p (g n) -> p g n", g=NG)
    inv = take(T)
    u = take(T)
    HALO = WINDOWS[-1] // 2
    GWP, GHP = GRID_W + 2 * HALO, GRID_H + 2 * HALO
    colbuf = [take(GRID_H * GWP).rearrange("p (r c) -> p r c", r=GRID_H) for _ in range(3)]
    rowbuf = [take(GHP * GRID_W).rearrange("p (r c) -> p r c", r=GHP) for _ in range(3)]
    ctxbuf = [take(CTX + 2 * HALO) for _ in range(3)]
    mean = take(T)

    def sync5(sp):
        sp.wait_ge(sem("scan_done"), H + 1)
        sp.wait_ge(sem("b_out"), 16 * H + 16)
        sp.dma_start(bT3, v["b_dram"].rearrange("(k p) t -> p k t", p=P)).then_inc(sem("b_in"), 16)
        for src, dst in ((w_in3[:, :, OFF_POOL:OFF_POOL + NG * P], w_pool), (a["pool_w"][0].rearrange("g c n -> c g n"), pool_w)):
            sp.dma_start(dst, src).then_inc(sem("pool_w_in"), 16)
        for g in range(NG):
            if g > 0:
                sp.wait_ge(sem("pool_in_ready"), g)
            sp.dma_start(inv, a["inv_count"][g:g + 1, :].to_broadcast([P, T])).then_inc(sem("inv_in"), 16)

    def pe5(pe):
        pe.wait_ge(sem("pool_w_in"), 32)

        def project(g):
            if g > 0:
                pe.wait_ge(sem("u_drained"), g)
            else:
                pe.wait_ge(sem("scan_done"), H + 1)
            for b, (at, n) in enumerate(COLS):
                for k in range(KD):
                    last = nc.tensor.matmul(banks[b][:, 0:n], w_pool[:, k, g * P:(g + 1) * P], hT3[:, k, at:at + n], start=(k == 0), stop=(k == KD - 1))
            last.then_inc(sem("u_filled"), 1)

        project(0)
        for g in range(NG):
            if g + 1 < NG:
                project(g + 1)
            pe.wait_ge(sem("pool_in_ready"), g + 1)
            if g > 0:
                pe.wait_ge(sem("p4_drained"), g)
            for b, (at, n) in enumerate(COLS):
                last = nc.tensor.matmul(banks[3 + b][:, 0:n], pool_w[:, g, :], mean[:, at:at + n], start=True, stop=True)
            last.then_inc(sem("p4_filled"), 1)

    def act5(act):
        def p4_out(g):
            act.wait_ge(sem("p4_filled"), g + 1)
            for b, (at, n) in enumerate(COLS):
                last = nc.scalar.activation(p4[:, g, at:at + n], banks[3 + b][:, 0:n], ACT.Copy, scale=cols[:, ROW_PSCALE + g:ROW_PSCALE + g + 1])
            last.then_inc(sem("p4_drained"), 1)

        act.wait_ge(*at_step("halo_zero"))
        for g in range(NG):
            act.wait_ge(sem("u_filled"), g + 1)
            if g > 0:
                act.wait_ge(sem("pool_in_ready"), g)
            for b, (at, n) in enumerate(COLS):
                nc.scalar.activation(u[:, at:at + n], banks[b][:, 0:n], ACT.Copy)
            nc.scalar.activation(ctxbuf[0][:, HALO:HALO + CTX], banks[0][:, 0:CTX], ACT.Copy)
            for b in range(2):
                last = nc.scalar.activation(colbuf[0][:, 8 * b:8 * b + 8, HALO:HALO + GRID_W], banks[1 + b][:, 0:512].rearrange("p (r c) -> p r c", c=GRID_W), ACT.Copy)
            last.then_inc(sem("u_drained"), 1)
            if g > 0:
                p4_out(g - 1)
        p4_out(NG - 1)

    def dve5(dve):
        n = [0]

        def step(ins):
            n[0] += 1
            ins.then_inc(sem("dve_pool"), 1)
            dve.wait_ge(sem("dve_pool"), n[0])

        nc.vector.memset(colbuf[0], 0.0)
        nc.vector.memset(rowbuf[0], 0.0)
        nc.vector.memset(ctxbuf[0], 0.0).then_inc(*reach("halo_zero"))
        for g, w in enumerate(WINDOWS):
            dve.wait_ge(sem("u_drained"), g + 1)
            m = w.bit_length() - 1
            src, width = colbuf[0], GWP
            for s in range(m):
                sh = 1 << s
                width -= sh
                if s == m - 1:
                    f = HALO - w // 2
                    step(nc.vector.tensor_tensor(rowbuf[0][:, HALO:HALO + GRID_H, :], src[:, :, f:f + GRID_W], src[:, :, f + sh:f + sh + GRID_W], ALU.add))
                else:
                    dst = colbuf[1 + s % 2]
                    step(nc.vector.tensor_tensor(dst[:, :, 0:width], src[:, :, 0:width], src[:, :, sh:sh + width], ALU.add))
                    src = dst
            src, rows = rowbuf[0], GHP
            for s in range(m):
                sh = 1 << s
                rows -= sh
                if s == m - 1:
                    f = HALO - w // 2
                    if g > 0:
                        dve.wait_ge(sem("p4_filled"), g)
                    step(nc.vector.tensor_tensor(mean[:, CTX:T].rearrange("p (r c) -> p r c", c=GRID_W), src[:, f:f + GRID_H, :], src[:, f + sh:f + sh + GRID_H, :], ALU.add))
                else:
                    dst = rowbuf[1 + s % 2]
                    step(nc.vector.tensor_tensor(dst[:, 0:rows, :], src[:, 0:rows, :], src[:, sh:sh + rows, :], ALU.add))
                    src = dst
            src, width = ctxbuf[0], CTX + 2 * HALO
            for s in range(m):
                sh = 1 << s
                width -= sh
                if s == m - 1:
                    f = HALO - w // 2
                    step(nc.vector.tensor_tensor(mean[:, 0:CTX], src[:, f:f + CTX], src[:, f + sh:f + sh + CTX], ALU.add))
                else:
                    dst = ctxbuf[1 + s % 2]
                    step(nc.vector.tensor_tensor(dst[:, 0:width], src[:, 0:width], src[:, sh:sh + width], ALU.add))
                    src = dst
            dve.wait_ge(sem("inv_in"), 16 * (g + 1))
            step(nc.vector.tensor_tensor(mean, mean, inv, ALU.mult))
            nc.vector.tensor_tensor(mean, mean, u, ALU.subtract).then_inc(sem("pool_in_ready"), 1)

    at_word[0] = MIX_AT
    mixT = take(KD * T)
    mixT3 = mixT.rearrange("p (k t) -> p k t", k=KD)
    w_outs = take(KD * D).rearrange("p (k n) -> p k n", k=KD)
    KB = 2 * KD + NG + KD
    w_mix = [take(KB * P).rearrange("p (k n) -> p k n", k=KB) for _ in range(2)]
    NTC = 3
    CH = T // NTC
    sg_all = v["mask_words"][:, 0:4 * CH].rearrange("p (s b c) -> p s b c", s=2, b=2)
    sg = [[sg_all[:, i, j, :] for j in range(2)] for i in range(2)]
    BR = ((0, KD), (KD, 2 * KD), (2 * KD, 2 * KD + NG), (2 * KD + NG, KB))

    def load_mix(sp, dt, s):
        for k0, src, col in ((0, w_in3, OFF_MERGE), (KD, w_in3, OFF_MERGE + D),
                             (2 * KD, a["pool_proj"][0].rearrange("(k p) n -> p k n", p=P), 0),
                             (2 * KD + NG, a["dn_proj"][0].rearrange("(k p) n -> p k n", p=P), 0)):
            nk = NG if k0 == 2 * KD else KD
            sp.dma_start(w_mix[s][:, k0:k0 + nk, :], src[:, :, bass.ds(dt * P + col, P)]).then_inc(sem(f"w_mix_in{s}"), 16)

    def sync6(sp):
        sp.wait_ge(sem("p4_drained"), NG)
        for s in range(2):
            load_mix(sp, s, s)
        with sp.Fori(0, KD // 2 - 1) as i:
            for s in range(2):
                sp.wait_ge(sem("mix_filled"), i * (2 * NTC) + (s + 1) * NTC)
                load_mix(sp, i * 2 + 2 + s, s)
        sp.dma_start(w_outs, a["w_out"][0].rearrange("(k p) n -> p k n", p=P)).then_inc(sem("w_out_in"), 16)

    def pe6(pe):
        srcs = (hT3, hT3, p4, bT3)
        pe.wait_ge(sem("b_in"), 16)
        pe.wait_ge(sem("p4_drained"), NG)
        with pe.Fori(0, KD // 2) as i:
            for s in range(2):
                pe.wait_ge(sem(f"w_mix_in{s}"), 64 * i + 64)
                for c in range(NTC):
                    n = s * NTC + c
                    st = n % 2
                    pe.wait_ge(sem("mix_drained"), i * (2 * NTC) + n + 1)
                    for br, (k0, k1) in enumerate(BR):
                        for k in range(k0, k1):
                            last = nc.tensor.matmul(banks[4 * st + br][:, 0:CH], w_mix[s][:, k, :], srcs[br][:, k - k0, c * CH:(c + 1) * CH], start=(k == k0), stop=(k == k1 - 1))
                    last.then_inc(sem("mix_filled"), 1)

    def act6(act):
        with act.Fori(0, KD // 2) as i:
            for n in range(2 * NTC):
                st = n % 2
                act.wait_ge(sem("mix_filled"), i * (2 * NTC) + n + 1)
                act.wait_ge(sem("mix_drained"), i * (2 * NTC) + n + 1)
                for br in range(2):
                    last = nc.scalar.activation(sg[st][br], banks[4 * st + br][:, 0:CH], ACT.Sigmoid)
                last.then_inc(sem("gates_ready"), 1)

    def dve6(dve):
        dve.wait_ge(sem("p4_drained"), NG)
        dve.sem_inc(sem("mix_drained"), 2)
        with dve.Fori(0, KD // 2) as i:
            for n in range(2 * NTC):
                st, s, c = n % 2, n // NTC, n % NTC
                dve.wait_ge(sem("gates_ready"), i * (2 * NTC) + n + 1)
                for br in range(2):
                    nc.vector.tensor_tensor(sg[st][br], sg[st][br], banks[4 * st + 2 + br][:, 0:CH], ALU.mult).then_inc(sem("mix_prod"), 1)
                dve.wait_ge(sem("mix_prod"), i * (4 * NTC) + 2 * n + 2)
                nc.vector.tensor_tensor(mixT[:, bass.ds((i * 2 + s) * T + c * CH, CH)], sg[st][0], sg[st][1], ALU.add).then_inc(sem("mix_drained"), 1)

    at_word[0] = PERSIST
    row = {n: [take(D) for _ in range(2)] for n in ("gate1", "amp2", "shift2")}
    norm2_row = take(D)
    router = take(KD * E).rearrange("p (k e) -> p k e", k=KD)
    assert at_word[0] <= BT_AT
    at_word[0] = BT_AT
    XR = 2
    x_t = [take(D) for _ in range(XR)]
    h2_t = [take(D) for _ in range(XR)]
    prod = [take(D) for _ in range(XR)]
    h2T = [take(D).rearrange("p (k t) -> p k t", k=KD) for _ in range(XR)]
    assert at_word[0] <= HEADS_AT
    st7 = small[:, 5:8]
    ssum = [small[:, 8 + i:9 + i] for i in range(2)]
    rstd = [small[:, 10 + i:11 + i] for i in range(2)]
    lnb = [small[:, 12 + i:13 + i] for i in range(2)]

    def x_tile(t):
        return a["x_prompt"][0] if t == 0 else a["x_sample"][0, (t - 1) * P:t * P, :]

    MIX_ALL = 2 * NTC * (KD // 2) + 2

    def sync7(sp):
        sp.wait_ge(sem("mix_drained"), MIX_ALL)
        for c in range(2):
            for i, n in ((2, "gate1"), (4, "amp2"), (3, "shift2")):
                sp.dma_start(row[n][c], mod_dram[c:c + 1, i * D:(i + 1) * D].to_broadcast([P, D])).then_inc(sem("rows_in"), 16)
        sp.dma_start(norm2_row, a["norm2_g"].to_broadcast([P, D])).then_inc(sem("rows_in"), 16)
        sp.dma_start(router, a["router_w"][0].rearrange("(k p) e -> p k e", p=P)).then_inc(sem("router_in"), 16)
        for t in range(XR):
            sp.dma_start(x_t[t % XR], x_tile(t)).then_inc(sem(f"xt_in{t % XR}"), 16)
        for t in range(NT):
            sp.wait_ge(sem("x1_ready"), t + 1)
            sp.dma_start(x2_dram[t * P:(t + 1) * P, :], x_t[t % XR]).then_inc(sem(f"x1_out{t % XR}"), 16)
            sp.wait_ge(sem("h2_ready"), t + 1)
            sp.dma_start(h2_dram[t * P:(t + 1) * P, :], h2_t[t % XR]).then_inc(sem(f"h2_out{t % XR}"), 16)
            if t + XR < NT:
                sp.wait_ge(sem(f"x1_out{t % XR}"), 16 * (t // XR + 1))
                sp.dma_start(x_t[t % XR], x_tile(t + XR)).then_inc(sem(f"xt_in{t % XR}"), 16)

    def pe7(pe):
        pe.wait_ge(sem("w_out_in"), 16)
        pe.wait_ge(sem("mix_drained"), MIX_ALL)

        def project(t):
            if t >= 2:
                pe.wait_ge(sem("y_drained"), t - 1)
            for half in range(2):
                for k in range(KD):
                    last = nc.tensor.matmul(banks[2 * (t % 2) + half][:, 0:512], mixT3[:, k, t * P:(t + 1) * P], w_outs[:, k, half * 512:(half + 1) * 512], start=(k == 0), stop=(k == KD - 1))
            last.then_inc(sem("y_filled"), 1)

        project(0)
        pe.wait_ge(sem("router_in"), 16)
        for t in range(NT):
            if t + 1 < NT:
                project(t + 1)
            pe.wait_ge(sem("h2_ready"), t + 1)
            if t > 0:
                pe.wait_ge(sem("h2T_ready"), t)
            for k in range(KD):
                last = nc.tensor.transpose(banks[4 + k // 4][:, (k % 4) * P:(k % 4 + 1) * P], h2_t[t % XR][:, k * P:(k + 1) * P], ident)
            last.then_inc(sem("h2T_filled"), 1)
            pe.wait_ge(sem("h2T_ready"), t + 1)
            for k in range(KD):
                last = nc.tensor.matmul(banks[6][:, t * E:(t + 1) * E], h2T[t % XR][:, k, :], router[:, k, :], start=(k == 0), stop=(k == KD - 1))
            last.then_inc(sem("logits_filled"), 1)

    def act7(act):
        for t in range(NT):
            act.wait_ge(sem("x1_ready"), t + 1)
            nc.scalar.activation(prod[t % XR], x_t[t % XR], ACT.Square, accum_out=ssum[t % 2]).then_inc(sem("act7"), 1)
            act.wait_ge(sem("act7"), 2 * t + 1)
            nc.scalar.activation(lnb[t % 2], ssum[t % 2], ACT.Ln, scale=1.0 / D, bias=eps_c).then_inc(sem("act7"), 1)
            act.wait_ge(sem("act7"), 2 * t + 2)
            nc.scalar.activation(rstd[t % 2], lnb[t % 2], ACT.Exp, scale=-0.5).then_inc(sem("rstd2"), 1)
            act.wait_ge(sem("h2T_filled"), t + 1)
            for i in range(2):
                last = nc.scalar.activation(h2T[t % XR][:, 4 * i:4 * i + 4, :].rearrange("p k t -> p (k t)"), banks[4 + i][:, 0:512], ACT.Copy)
            last.then_inc(sem("h2T_ready"), 1)

    def dve7(dve):
        dve.wait_ge(sem("rows_in"), 16 * 7)
        for c in range(2):
            last = nc.vector.scalar_tensor_tensor(row["amp2"][c], row["amp2"][c], 1.0, norm2_row, ALU.add, ALU.mult)
        last.then_inc(*reach("amp2_ready"))
        dve.wait_ge(*at_step("amp2_ready"))
        for t in range(NT):
            c, s = min(t, 1), t % XR
            dve.wait_ge(sem("y_filled"), t + 1)
            if t >= 2:
                dve.wait_ge(sem("rstd2"), t - 1)
            for half in range(2):
                last = nc.vector.tensor_tensor(prod[s][:, half * 512:(half + 1) * 512], banks[2 * (t % 2) + half][:, 0:512], row["gate1"][c][:, half * 512:(half + 1) * 512], ALU.mult)
            last.then_inc(sem("y_drained"), 1)
            dve.wait_ge(sem("y_drained"), t + 1)
            dve.wait_ge(sem(f"xt_in{s}"), 16 * (t // XR + 1))
            nc.vector.tensor_tensor(x_t[s], x_t[s], prod[s], ALU.add).then_inc(sem("x1_ready"), 1)
            dve.wait_ge(sem("rstd2"), t + 1)
            if t >= XR:
                dve.wait_ge(sem(f"h2_out{s}"), 16 * (t // XR))
                dve.wait_ge(sem("h2T_filled"), t - 1)
            nc.vector.scalar_tensor_tensor(h2_t[s], x_t[s], rstd[t % 2], row["amp2"][c], ALU.mult, ALU.mult).then_inc(sem("h2_scaled"), 1)
            dve.wait_ge(sem("h2_scaled"), t + 1)
            nc.vector.tensor_tensor(h2_t[s], h2_t[s], row["shift2"][c], ALU.add).then_inc(sem("h2_ready"), 1)

    at_word[0] = PERSIST
    routing = {n: take(NT * E) for n in ("logit", "aff")}
    mx, sm = take(NT), take(NT)
    affT = take(T)
    work = take(T)
    vals, idxu, idxf = take(CAP), take(CAP).bitcast(U32), take(CAP)
    gates_l, gates_c, idx_l, idx_c = take(E), take(E), take(E).bitcast(U32), take(E).bitcast(U32)
    idx_now = [take(4).bitcast(U32) for _ in range(2)]
    ROUTE_END = at_word[0]
    lg3 = routing["logit"].rearrange("p (t e) -> p t e", t=NT)
    af3 = routing["aff"].rearrange("p (t e) -> p t e", t=NT)

    def dve8(dve):
        n = [0]

        def step(ins):
            n[0] += 1
            ins.then_inc(sem("dve_route"), 1)
            dve.wait_ge(sem("dve_route"), n[0])

        dve.wait_ge(sem("logits_filled"), NT)
        lps = banks[6][:, 0:NT * E].rearrange("p (t e) -> p t e", t=NT)
        step(nc.vector.tensor_reduce(mx, lps, AX_X, ALU.max))
        nc.vector.tensor_tensor(lg3, lps, mx.unsqueeze(2).to_broadcast([P, NT, E]), ALU.subtract).then_inc(*reach("route_shift"))
        dve.wait_ge(*at_step("route_exp"))
        step(nc.vector.tensor_reduce(sm, af3, AX_X, ALU.add))
        step(nc.vector.reciprocal(sm, sm))
        nc.vector.tensor_tensor(af3, af3, sm.unsqueeze(2).to_broadcast([P, NT, E]), ALU.mult).then_inc(*reach("aff_ready"))
        dve.wait_ge(*at_step("affT_filled"))
        for b in range(3):
            last = nc.vector.tensor_copy(affT[0:E, b * 384:(b + 1) * 384], banks[b][0:E, 0:384])
        step(last)
        for at, n_tok, cap, col in ((CTX, LAT, CAP_L, 0), (0, CTX, CAP_C, CAP_L)):
            row_ = affT[0:E, at:at + n_tok]
            for r in range(cap // 8):
                o = col + 8 * r
                step(nc.vector.max(vals[0:E, o:o + 8], row_))
                step(nc.vector.max_index(idxu[0:E, o:o + 8], vals[0:E, o:o + 8], row_))
                if r < cap // 8 - 1:
                    step(nc.vector.match_replace(row_, vals[0:E, o:o + 8], row_, -1.0))
        step(nc.vector.tensor_copy(idxf[0:E, :], idxu[0:E, :]))
        nc.vector.tensor_scalar(idxf[0:E, 0:CAP_L], idxf[0:E, 0:CAP_L], float(CTX), None, ALU.add).then_inc(*reach("topk_ready"))
        dve.wait_ge(*at_step("topkT_filled"))
        nc.vector.tensor_copy(gates_l, banks[3][:, 0:E])
        nc.vector.tensor_copy(gates_c[0:CAP_C, :], banks[3][0:CAP_C, E:2 * E])
        nc.vector.tensor_copy(idx_l, banks[3][:, 2 * E:3 * E])
        nc.vector.tensor_copy(idx_c[0:CAP_C, :], banks[3][0:CAP_C, 3 * E:4 * E]).then_inc(*reach("routes_ready"))

    def act8(act):
        act.wait_ge(*at_step("route_shift"))
        nc.scalar.activation(routing["aff"], routing["logit"], ACT.Exp).then_inc(*reach("route_exp"))

    def pe8(pe):
        pe.wait_ge(*at_step("aff_ready"))
        for t in range(NT):
            last = nc.tensor.transpose(banks[t // 3][0:E, (t % 3) * P:(t % 3 + 1) * P], af3[:, t, :], ident)
        last.then_inc(*reach("affT_filled"))
        pe.wait_ge(*at_step("topk_ready"))
        nc.tensor.transpose(banks[3][:, 0:E], vals[0:E, 0:CAP_L], ident[0:E, 0:E])
        nc.tensor.transpose(banks[3][0:CAP_C, E:2 * E], vals[0:E, CAP_L:CAP], ident[0:E, 0:E])
        nc.tensor.transpose(banks[3][:, 2 * E:3 * E], idxf[0:E, 0:CAP_L], ident[0:E, 0:E])
        nc.tensor.transpose(banks[3][0:CAP_C, 3 * E:4 * E], idxf[0:E, CAP_L:CAP], ident[0:E, 0:E]).then_inc(*reach("topkT_filled"))

    NU = 6
    HALF = D // 2
    w_unit = [take(KD * HALF).rearrange("p (k n) -> p k n", k=KD) for _ in range(NU)]
    xs_l, xs_c = take(D), take(D)
    xsT = take(KD * CAP).rearrange("p (k c) -> p k c", k=KD)
    hid = take(KD * CAP).rearrange("p (k c) -> p k c", k=KD)
    sil = [take(CAP) for _ in range(2)]
    ysT = take(KD * CAP).rearrange("p (k c) -> p k c", k=KD)
    ys_l, ys_c = take(D), take(D)
    WMATS = ((0, 0), (1, 0), (0, 1), (1, 1), (2, 0), (2, 1))

    def load_unit(sp, e, u_):
        m, half = WMATS[u_]
        src = a[("exp_w_gate", "exp_w_up", "exp_w_down")[m]][0].rearrange("e k n -> (e k) n")[bass.ds(e * D, D), half * HALF:(half + 1) * HALF]
        sp.dma_start(w_unit[u_], src.rearrange("(k p) n -> p k n", p=P)).then_inc(sem(f"unit_in{u_}"), 16)

    def sync9(sp):
        sp.wait_ge(sem("logits_filled"), NT)
        for s in range(XR):
            n_s = len(range(s, NT, XR))
            sp.wait_ge(sem(f"x1_out{s}"), 16 * n_s)
            sp.wait_ge(sem(f"h2_out{s}"), 16 * n_s)
        for u_ in range(NU):
            load_unit(sp, 0, u_)
        with sp.Fori(0, E - 1) as e:
            for name, units in (("gu_filled", (0, 1, 2, 3)), ("dn_filled", (4, 5))):
                for u_ in units:
                    half = WMATS[u_][1]
                    sp.wait_ge(sem(name), e * KD + (half + 1) * (KD // 2))
                    load_unit(sp, e + 1, u_)

    def gather(pool, e):
        pool.wait_ge(sem("gather_idx"), e + 1)
        alone(pool)
        nc.gpsimd.indirect_dma_start(xs_l, None, h2_dram, bass.IndirectOffsetOnAxis(ap=idx_now[0][:, 0:1], axis=0)).then_inc(sem("xs_in"), 16)
        nc.gpsimd.indirect_dma_start(xs_c[0:CAP_C, :], None, h2_dram, bass.IndirectOffsetOnAxis(ap=idx_now[0][0:CAP_C, 1:2], axis=0)).then_inc(sem("xs_in"), 16)

    def scatter(pool, e):
        pool.wait_ge(sem("ys_ready"), e + 1)
        alone(pool)
        nc.gpsimd.indirect_dma_start(x2_dram, bass.IndirectOffsetOnAxis(ap=idx_now[1][:, 0:1], axis=0), ys_l, None, compute_op=ALU.add).then_inc(sem("scattered"), 16)
        nc.gpsimd.indirect_dma_start(x2_dram, bass.IndirectOffsetOnAxis(ap=idx_now[1][0:CAP_C, 1:2], axis=0), ys_c[0:CAP_C, :], None, compute_op=ALU.add).then_inc(sem("scattered"), 16)
        pool.wait_ge(sem("scattered"), e * 32 + 32)
        alone(pool)
        nc.gpsimd.memset(small[:, 3:4], 0.0).then_inc(sem("scatter_free"), 1)

    def pool9(pool):
        for s in range(XR):
            n_s = len(range(s, NT, XR))
            pool.wait_ge(sem(f"x1_out{s}"), 16 * n_s)
            pool.wait_ge(sem(f"h2_out{s}"), 16 * n_s)
        pool.sem_inc(sem("scatter_free"), 1)
        gather(pool, 0)
        gather(pool, 1)
        with pool.Fori(1, E - 1) as e:
            gather(pool, e + 1)
            scatter(pool, e - 1)
        scatter(pool, E - 2)
        scatter(pool, E - 1)

    def turn_in(pe, e, first=False):
        pe.wait_ge(sem("xs_in"), 32 * e + 32)
        if not first:
            pe.wait_ge(sem("ysT_drained"), e - 1)
        for k in range(KD):
            o = (k % 3) * CAP
            nc.tensor.transpose(banks[k // 3][:, o:o + CAP_L], xs_l[:, k * P:(k + 1) * P], ident)
            last = nc.tensor.transpose(banks[k // 3][:, o + CAP_L:o + CAP], xs_c[0:CAP_C, k * P:(k + 1) * P], ident[0:CAP_C, 0:CAP_C])
        last.then_inc(sem("xsT_filled"), 1)

    def turn_out(pe, e):
        pe.wait_ge(sem("dn_drained"), e * KD + KD + 2)
        for dt in range(KD):
            o = (dt % 4) * P
            nc.tensor.transpose(banks[dt // 4][:, o:o + P], ysT[:, dt, 0:CAP_L], ident)
            last = nc.tensor.transpose(banks[(2, 7)[dt // 4]][0:CAP_C, o:o + P], ysT[:, dt, CAP_L:CAP], ident)
        last.then_inc(sem("ysT_filled"), 1)

    def body9_pe(pe, e, first=False, last_e=False):
        pe.wait_ge(sem("xsT_ready"), e + 1)
        for f in range(KD):
            half, col = f // 4, (f % 4) * P
            if f % 4 == 0:
                pe.wait_ge(sem(f"unit_in{2 * half}"), 16 * e + 16)
                pe.wait_ge(sem(f"unit_in{2 * half + 1}"), 16 * e + 16)
            pe.wait_ge(sem("gu_drained"), e * KD + f + 1)
            for m in range(2):
                for k in range(KD):
                    last = nc.tensor.matmul(banks[3 + f % 2][:, m * CAP:(m + 1) * CAP], w_unit[2 * half + m][:, k, col:col + P], xsT[:, k, :], start=(k == 0), stop=(k == KD - 1))
            last.then_inc(sem("gu_filled"), 1)
            if f == 1 and not first:
                turn_out(pe, e - 1)
        if not last_e:
            turn_in(pe, e + 1, first)
        for dt in range(KD):
            half, col = dt // 4, (dt % 4) * P
            if dt == 0:
                pe.wait_ge(sem("gu_drained"), e * KD + KD + 2)
            if dt % 4 == 0:
                pe.wait_ge(sem(f"unit_in{4 + half}"), 16 * e + 16)
            pe.wait_ge(sem("dn_drained"), e * KD + dt + 1)
            for k in range(KD):
                last = nc.tensor.matmul(banks[5 + dt % 2][:, 0:CAP], w_unit[4 + half][:, k, col:col + P], hid[:, k, :], start=(k == 0), stop=(k == KD - 1))
            last.then_inc(sem("dn_filled"), 1)

    def pe9(pe):
        turn_in(pe, 0, True)
        body9_pe(pe, 0, first=True)
        with pe.Fori(1, E - 1) as e:
            body9_pe(pe, e)
        body9_pe(pe, E - 1, last_e=True)
        turn_out(pe, E - 1)

    def evac_in(act, e):
        act.wait_ge(sem("xsT_filled"), e + 1)
        for b, nk in ((0, 3), (1, 3), (2, 2)):
            last = nc.scalar.activation(xsT[:, 3 * b:3 * b + nk, :].rearrange("p k c -> p (k c)"), banks[b][:, 0:nk * CAP], ACT.Copy)
        last.then_inc(sem("xsT_ready"), 1)

    def body9_act(act, e, last_e=False):
        for f in range(KD):
            act.wait_ge(sem("gu_filled"), e * KD + f + 1)
            nc.scalar.activation(sil[f % 2], banks[3 + f % 2][:, 0:CAP], ACT.Silu).then_inc(sem("sil_ready"), 1)
        if not last_e:
            evac_in(act, e + 1)
        for dt in range(KD):
            act.wait_ge(sem("dn_filled"), e * KD + dt + 1)
            nc.scalar.activation(ysT[:, dt, 0:CAP_L], banks[5 + dt % 2][:, 0:CAP_L], ACT.Copy, scale=modT3[:, 1, 5 * KD + dt:5 * KD + dt + 1])
            nc.scalar.activation(ysT[:, dt, CAP_L:CAP], banks[5 + dt % 2][:, CAP_L:CAP], ACT.Copy, scale=modT3[:, 0, 5 * KD + dt:5 * KD + dt + 1]).then_inc(sem("dn_drained"), 1)

    def act9(act):
        act.wait_ge(*at_step("gate2_ready"))
        evac_in(act, 0)
        with act.Fori(0, E - 1) as e:
            body9_act(act, e)
        body9_act(act, E - 1, True)

    def set_gather_idx(e):
        nc.vector.tensor_copy(idx_now[0][:, 0:1], idx_l[:, bass.ds(e, 1)])
        nc.vector.tensor_copy(idx_now[0][0:CAP_C, 1:2], idx_c[0:CAP_C, bass.ds(e, 1)]).then_inc(sem("gather_idx"), 1)

    def weigh(dve, e):
        dve.wait_ge(sem("ysT_filled"), e + 1)
        dve.wait_ge(sem("scatter_free"), e + 1)
        nc.vector.tensor_copy(idx_now[1][:, 0:1], idx_l[:, bass.ds(e, 1)])
        nc.vector.tensor_copy(idx_now[1][0:CAP_C, 1:2], idx_c[0:CAP_C, bass.ds(e, 1)])
        for half in range(2):
            nc.vector.tensor_scalar(ys_l[:, half * 512:(half + 1) * 512], banks[half][:, 0:512], gates_l[:, bass.ds(e, 1)], None, ALU.mult)
        for half in range(2):
            last = nc.vector.tensor_scalar(ys_c[0:CAP_C, half * 512:(half + 1) * 512], banks[(2, 7)[half]][0:CAP_C, 0:512], gates_c[0:CAP_C, bass.ds(e, 1)], None, ALU.mult)
        last.then_inc(sem("ys_ready"), 1)
        nc.vector.memset(small[:, 4:5], 0.0).then_inc(sem("ysT_drained"), 1)

    def body9_dve(dve, e, first=False, last_e=False):
        if not last_e:
            dve.wait_ge(sem("xsT_filled"), e + 1)
            set_gather_idx(e + 1)
        for f in range(KD):
            dve.wait_ge(sem("sil_ready"), e * KD + f + 1)
            nc.vector.tensor_tensor(hid[:, f, :], sil[f % 2], banks[3 + f % 2][:, CAP:2 * CAP], ALU.mult).then_inc(sem("gu_drained"), 1)
            if f == 2 and not first:
                weigh(dve, e - 1)

    def dve9(dve):
        for name, k in (("gu_drained", 2), ("dn_drained", 2)):
            dve.sem_inc(sem(name), k)
        dve.wait_ge(*at_step("routes_ready"))
        set_gather_idx(0)
        body9_dve(dve, 0, first=True)
        with dve.Fori(1, E - 1) as e:
            body9_dve(dve, e)
        body9_dve(dve, E - 1, last_e=True)
        weigh(dve, E - 1)

    at_word[0] = ROUTE_END
    fin_row = take(D)
    xf = [take(D) for _ in range(3)]
    yf = [take(D) for _ in range(3)]
    sqf = take(D)
    fss, fln, frs = take(NT), take(NT), take(NT)

    def sync10(sp):
        sp.wait_ge(sem("scattered"), 32 * E)
        sp.dma_start(fin_row, a["final_norm_g"].rearrange("(o d) -> o d", o=1).to_broadcast([P, D])).then_inc(sem("fin_in"), 16)
        for t in range(NT):
            if t >= 3:
                sp.wait_ge(sem("yf_ready"), t - 2)
            sp.dma_start(xf[t % 3], x2_dram[t * P:(t + 1) * P, :]).then_inc(sem(f"xf_in{t % 3}"), 16)
            if t >= 2:
                store_y(sp, t - 2)
        store_y(sp, NT - 2)
        store_y(sp, NT - 1)
        for s in range(3):
            sp.wait_ge(sem(f"y_out{s}"), 16 * 3)
        for d in range(2):
            sp.wait_ge(sem(f"S_out{d}"), 16 * H)

    def store_y(sp, t):
        dst = out_p[0] if t == 0 else out_s[0, (t - 1) * P:t * P, :]
        sp.wait_ge(sem("yf_ready"), t + 1)
        sp.dma_start(dst, yf[t % 3]).then_inc(sem(f"y_out{t % 3}"), 16)

    def act10(act):
        for t in range(NT):
            act.wait_ge(sem(f"xf_in{t % 3}"), 16 * (t // 3 + 1))
            nc.scalar.activation(sqf, xf[t % 3], ACT.Square, accum_out=fss[:, t:t + 1]).then_inc(sem("act10"), 1)
            act.wait_ge(sem("act10"), 2 * t + 1)
            nc.scalar.activation(fln[:, t:t + 1], fss[:, t:t + 1], ACT.Ln, scale=1.0 / D, bias=eps_c).then_inc(sem("act10"), 1)
            act.wait_ge(sem("act10"), 2 * t + 2)
            nc.scalar.activation(frs[:, t:t + 1], fln[:, t:t + 1], ACT.Exp, scale=-0.5).then_inc(sem("frs_ready"), 1)

    def dve10(dve):
        dve.wait_ge(sem("fin_in"), 16)
        for t in range(NT):
            dve.wait_ge(sem("frs_ready"), t + 1)
            if t >= 3:
                dve.wait_ge(sem(f"y_out{t % 3}"), 16 * (t // 3))
            nc.vector.scalar_tensor_tensor(yf[t % 3], xf[t % 3], frs[:, t:t + 1], fin_row, ALU.mult, ALU.mult).then_inc(sem("yf_ready"), 1)

    def f_sync(sp):
        if stop >= 5:
            sync5(sp)
        if stop >= 6:
            sync6(sp)
            sync7(sp)
        if stop >= 9:
            sync9(sp)
            sync10(sp)

    def f_pe(pe):
        if stop >= 5:
            pe5(pe)
        if stop >= 6:
            pe6(pe)
            pe7(pe)
        if stop >= 8:
            pe8(pe)
        if stop >= 9:
            pe9(pe)

    def f_act(act):
        if stop >= 5:
            act5(act)
        if stop >= 6:
            act6(act)
            act7(act)
        if stop >= 8:
            act8(act)
        if stop >= 9:
            act9(act)
            act10(act)

    def f_dve(dve):
        if stop >= 5:
            dve5(dve)
        if stop >= 6:
            dve6(dve)
            dve7(dve)
        if stop >= 8:
            dve8(dve)
        if stop >= 9:
            dve9(dve)
            dve10(dve)

    def f_pool(pool):
        if stop >= 9:
            pool9(pool)

    return {"sync": f_sync, "tensor": f_pe, "scalar": f_act, "vector": f_dve, "gpsimd": f_pool, **{"bT": bT}}


_INS = ["x_prompt", "x_sample", "state_dn_fwd", "state_dn_bwd", "c", "c_ctx", "ada_w", "ada_b", "norm1_g",
        "norm2_g", "w_in", "pool_w", "pool_scale", "pool_proj", "dn_conv", "dn_a_log", "dn_dt_bias",
        "dn_onorm_g", "dn_proj", "w_out", "router_w", "exp_w_gate", "exp_w_up", "exp_w_down", "final_norm_g"]
_OUTS = [(1, CTX, D), (1, LAT, D), (1, 1, H, P, P), (1, 1, H, P, P)]


def shape_constants():
    i = np.arange(P)
    r, c = i[:, None], i[None, :]
    consts = np.stack([r == c, np.ones((P, P)), r <= c, r >= c]).astype(np.float32)
    masks = np.zeros((2, 7, P, P), np.uint32)
    for lv in range(7):
        b = 1 << lv
        masks[0, lv] = (r // b % 2 == 1) & (c // b == r // b - 1)
        masks[1, lv] = masks[0, lv].T
    inv = np.zeros((NG, T), np.float32)

    def counts(n, w):
        t = np.arange(n)
        return np.clip(t + w // 2, 0, n) - np.clip(t - w // 2, 0, n)

    for g, w in enumerate(WINDOWS):
        inv[g, :CTX] = 1.0 / counts(CTX, w)
        inv[g, CTX:] = (1.0 / (counts(GRID_H, w)[:, None] * counts(GRID_W, w)[None, :])).ravel()
    return {"consts": consts, "masks": masks, "inv_count": inv}


def kernel(**inputs):
    import concourse.bacc as bacc
    from concourse.bass_utils import run_bass_kernel_spmd

    nc = bacc.Bacc("TRN2", target_bir_lowering=False, num_devices=1)
    arrays, a = {}, {}
    given = {n: np.ascontiguousarray(inputs[n]) for n in _INS} | shape_constants()
    for name, x in given.items():
        arrays[f"in_{name}"] = x
        a[name] = nc.dram_tensor(f"in_{name}", x.shape, mybir.dt.from_np(x.dtype), kind="ExternalInput").ap()
    outs = [nc.dram_tensor(f"out_{i}", s, F32, kind="ExternalOutput").ap() for i, s in enumerate(_OUTS)]
    build(nc, a, *outs)
    r = run_bass_kernel_spmd(nc, [arrays], core_ids=[0])
    return tuple(r.results[0][f"out_{i}"] for i in range(len(_OUTS)))
```
